# Optimizing a Trainium2 kernel written in Bass

```python
import jax, jax.numpy as jnp
from jax import lax
import numpy as np
import math

D_MODEL = 1024
BATCH = 1
SEQ = 256
DEPTH = 1

MEM_LEN = 256
D_CONV = D_MODEL
CONV_KERNEL = 31
D_SHORT = D_MODEL
SHORT_KERNEL = 3
D_POOL = D_MODEL
POOL_WINDOWS = (2, 4, 8, 16)
N_POOL_GROUPS = 4
POOL_GROUP = D_POOL // N_POOL_GROUPS
N_BRANCHES = 3
D_IN_PROJ = 2 * D_CONV + 3 * D_SHORT + D_POOL + N_BRANCHES * D_MODEL
N_XHEADS = 4
XHEAD_DIM = D_MODEL // N_XHEADS
N_EXPERTS = 32
TOP_K = 4
D_EXPERT = D_MODEL
SWIGLU_LIMIT = 7.0
SWIGLU_ALPHA = 1.702
EXPERT_BLOCK = 128
DEEPNORM_ALPHA = float((2 * DEPTH) ** 0.25)
DEEPNORM_BETA = float((8 * DEPTH) ** -0.25)
LN_EPS = 1e-5


def layer_norm(x, g, b):
    xf = x.astype(jnp.float32)
    mu = jnp.mean(xf, axis=-1, keepdims=True)
    var = jnp.mean(jnp.square(xf - mu), axis=-1, keepdims=True)
    y = (xf - mu) * lax.rsqrt(var + LN_EPS)
    return (y * g + b).astype(x.dtype)

def causal_depthwise_conv(u, w):
    k_width, ch = w.shape
    return lax.conv_general_dilated(
        u, w[:, None, :].astype(u.dtype), window_strides=(1,), padding=[(k_width - 1, 0)],
        dimension_numbers=("NWC", "WIO", "NWC"), feature_group_count=ch)

def causal_multiscale_pool(u):
    bsz, t_len, _ = u.shape
    uf = u.astype(jnp.float32).reshape(bsz, t_len, N_POOL_GROUPS, POOL_GROUP)
    cs = jnp.cumsum(uf, axis=1)
    pos = jnp.arange(t_len)
    outs = []
    for gi, win in enumerate(POOL_WINDOWS):
        c = cs[:, :, gi]
        prev = jnp.pad(c, ((0, 0), (win, 0), (0, 0)))[:, :t_len]
        cnt = jnp.minimum(pos + 1, win).astype(jnp.float32)
        outs.append((c - prev) / cnt[None, :, None])
    pooled = jnp.stack(outs, axis=2)
    return (pooled - uf).astype(u.dtype)

def mixer_sublayer(x, w_in, b_in, conv_a_w, conv_a_b, ln_a_g, ln_a_b, w_a_out, b_a_out,
                   conv_b_w, w_b_out, pool_w, pool_scale, w_mix_out):
    bsz, t_len, _ = x.shape
    p = x @ w_in + b_in
    o1 = 2 * D_CONV
    o2 = o1 + D_SHORT
    o3 = o2 + D_SHORT
    o4 = o3 + D_SHORT
    o5 = o4 + D_POOL
    a_in, gate_b, gate_c, v_bc, pool_in, gates = (
        p[..., :o1], p[..., o1:o2], p[..., o2:o3], p[..., o3:o4], p[..., o4:o5], p[..., o5:])
    a = a_in[..., :D_CONV] * jax.nn.sigmoid(a_in[..., D_CONV:])
    a = causal_depthwise_conv(a, conv_a_w) + conv_a_b
    a = jax.nn.silu(layer_norm(a, ln_a_g, ln_a_b))
    y_a = a @ w_a_out + b_a_out
    u = causal_depthwise_conv(gate_c * v_bc, conv_b_w)
    y_b = (gate_b * u) @ w_b_out
    pooled = causal_multiscale_pool(pool_in)
    y_c = jnp.einsum("btgc,gcd->btgd", pooled, pool_w).reshape(bsz, t_len, D_POOL) * pool_scale
    g_a = gates[..., :D_MODEL]
    g_b = gates[..., D_MODEL:2 * D_MODEL]
    g_c = gates[..., 2 * D_MODEL:]
    m = jax.nn.sigmoid(g_a) * y_a + jax.nn.sigmoid(g_b) * y_b + jax.nn.sigmoid(g_c) * y_c
    return m @ w_mix_out

def memory_cross_attention(x, mem_n, w_q, w_k, w_v, w_o):
    bsz, t_len, d = x.shape
    m_len = mem_n.shape[1]
    q = (x @ w_q).reshape(bsz, t_len, N_XHEADS, XHEAD_DIM)
    k = (mem_n @ w_k).reshape(bsz, m_len, N_XHEADS, XHEAD_DIM)
    v = (mem_n @ w_v).reshape(bsz, m_len, N_XHEADS, XHEAD_DIM)
    s = jnp.einsum("bshk,bmhk->bhsm", q.astype(jnp.float32), k.astype(jnp.float32)) * (XHEAD_DIM ** -0.5)
    prob = jax.nn.softmax(s, axis=-1).astype(v.dtype)
    o = jnp.einsum("bhsm,bmhk->bshk", prob, v).reshape(bsz, t_len, d)
    return o @ w_o

def clamped_swiglu(gu):
    gate = jnp.minimum(gu[..., :D_EXPERT], SWIGLU_LIMIT)
    up = jnp.clip(gu[..., D_EXPERT:], -SWIGLU_LIMIT, SWIGLU_LIMIT)
    return (up + 1.0) * (gate * jax.nn.sigmoid(gate * SWIGLU_ALPHA))

def moe_sublayer(h, router_w, router_b, w_gu, b_gu, w_down, b_down):
    bsz, t_len, d = h.shape
    n_tok = bsz * t_len
    hf = h.reshape(n_tok, d)
    logits = (hf @ router_w).astype(jnp.float32) + router_b.astype(jnp.float32)
    top_logits, top_idx = lax.top_k(logits, TOP_K)
    gates = jax.nn.softmax(top_logits, axis=-1)
    n_assign = n_tok * TOP_K
    flat_e = top_idx.reshape(n_assign).astype(jnp.int32)
    flat_tok = jnp.arange(n_assign, dtype=jnp.int32) // TOP_K
    flat_gate = gates.reshape(n_assign)
    order = jnp.argsort(flat_e)
    e_sorted = flat_e[order]
    counts = jnp.bincount(flat_e, length=N_EXPERTS).astype(jnp.int32)
    padded = ((counts + EXPERT_BLOCK - 1) // EXPERT_BLOCK) * EXPERT_BLOCK
    pad_end = jnp.cumsum(padded)
    pad_start = pad_end - padded
    grp_start = jnp.cumsum(counts) - counts
    dest = pad_start[e_sorted] + (jnp.arange(n_assign, dtype=jnp.int32) - grp_start[e_sorted])
    n_blocks = (n_assign + N_EXPERTS * (EXPERT_BLOCK - 1) + EXPERT_BLOCK - 1) // EXPERT_BLOCK
    n_rows = n_blocks * EXPERT_BLOCK
    row_tok = jnp.full((n_rows,), n_tok, jnp.int32).at[dest].set(flat_tok[order])
    row_gate = jnp.zeros((n_rows,), jnp.float32).at[dest].set(flat_gate[order])
    block_start = jnp.arange(n_blocks, dtype=jnp.int32) * EXPERT_BLOCK
    block_e = jnp.minimum(jnp.searchsorted(pad_end, block_start, side="right"), N_EXPERTS - 1)
    h_pad = jnp.concatenate([hf, jnp.zeros((1, d), hf.dtype)], axis=0)

    def step(acc, blk):
        tok, g, e = blk
        xb = h_pad[tok]
        act = clamped_swiglu(xb @ w_gu[e] + b_gu[e])
        yb = act @ w_down[e] + b_down[e]
        return acc.at[tok].add(yb * g[:, None].astype(yb.dtype)), None

    acc0 = jnp.zeros((n_tok + 1, d), h.dtype)
    acc, _ = lax.scan(step, acc0, (row_tok.reshape(n_blocks, EXPERT_BLOCK),
                                   row_gate.reshape(n_blocks, EXPERT_BLOCK), block_e))
    return acc[:n_tok].reshape(bsz, t_len, d)

def first_inputs(seed: int = 0) -> dict:
    key = jax.random.key(seed)
    ks = jax.random.split(key, 40)
    L = DEPTH
    f32 = jnp.float32

    def nrm(k, shape, scale):
        return jax.random.normal(k, shape, f32) * scale

    def gain(k, shape):
        return 1.0 + 0.05 * jax.random.normal(k, shape, f32)

    def bias(k, shape, scale=0.02):
        return scale * jax.random.normal(k, shape, f32)

    return {
        "x": nrm(ks[0], (BATCH, SEQ, D_MODEL), 1.0),
        "mem": nrm(ks[1], (BATCH, MEM_LEN, D_MODEL), 1.0),
        "mem_ln_g": gain(ks[2], (D_MODEL,)),
        "mem_ln_b": bias(ks[3], (D_MODEL,)),
        "w_in": nrm(ks[4], (L, D_MODEL, D_IN_PROJ), D_MODEL ** -0.5),
        "b_in": bias(ks[5], (L, D_IN_PROJ)),
        "conv_a_w": nrm(ks[6], (L, CONV_KERNEL, D_CONV), CONV_KERNEL ** -0.5),
        "conv_a_b": bias(ks[7], (L, D_CONV)),
        "ln_a_g": gain(ks[8], (L, D_CONV)),
        "ln_a_b": bias(ks[9], (L, D_CONV)),
        "w_a_out": nrm(ks[10], (L, D_CONV, D_MODEL), D_CONV ** -0.5),
        "b_a_out": bias(ks[11], (L, D_MODEL)),
        "conv_b_w": nrm(ks[12], (L, SHORT_KERNEL, D_SHORT), SHORT_KERNEL ** -0.5),
        "w_b_out": nrm(ks[13], (L, D_SHORT, D_MODEL), D_SHORT ** -0.5),
        "pool_w": nrm(ks[14], (L, N_POOL_GROUPS, POOL_GROUP, POOL_GROUP), POOL_GROUP ** -0.5),
        "pool_scale": gain(ks[15], (L, D_POOL)),
        "w_mix_out": nrm(ks[16], (L, D_MODEL, D_MODEL), DEEPNORM_BETA * D_MODEL ** -0.5),
        "ln1_g": gain(ks[17], (L, D_MODEL)),
        "ln1_b": bias(ks[18], (L, D_MODEL)),
        "w_xq": nrm(ks[19], (L, D_MODEL, D_MODEL), D_MODEL ** -0.5),
        "w_xk": nrm(ks[20], (L, D_MODEL, D_MODEL), D_MODEL ** -0.5),
        "w_xv": nrm(ks[21], (L, D_MODEL, D_MODEL), DEEPNORM_BETA * D_MODEL ** -0.5),
        "w_xo": nrm(ks[22], (L, D_MODEL, D_MODEL), DEEPNORM_BETA * D_MODEL ** -0.5),
        "ln2_g": gain(ks[23], (L, D_MODEL)),
        "ln2_b": bias(ks[24], (L, D_MODEL)),
        "router_w": nrm(ks[25], (L, D_MODEL, N_EXPERTS), D_MODEL ** -0.5),
        "router_b": bias(ks[26], (L, N_EXPERTS), 0.01),
        "w_gu": nrm(ks[27], (L, N_EXPERTS, D_MODEL, 2 * D_EXPERT), D_MODEL ** -0.5),
        "b_gu": bias(ks[28], (L, N_EXPERTS, 2 * D_EXPERT), 0.01),
        "w_down": nrm(ks[29], (L, N_EXPERTS, D_EXPERT, D_MODEL), DEEPNORM_BETA * D_EXPERT ** -0.5),
        "b_down": bias(ks[30], (L, N_EXPERTS, D_MODEL), 0.01),
        "ln3_g": gain(ks[31], (L, D_MODEL)),
        "ln3_b": bias(ks[32], (L, D_MODEL)),
    }

def first_block(x, mem, mem_ln_g, mem_ln_b, w_in, b_in, conv_a_w, conv_a_b, ln_a_g, ln_a_b,
              w_a_out, b_a_out, conv_b_w, w_b_out, pool_w, pool_scale, w_mix_out, ln1_g, ln1_b,
              w_xq, w_xk, w_xv, w_xo, ln2_g, ln2_b, router_w, router_b, w_gu, b_gu, w_down,
              b_down, ln3_g, ln3_b):
    mem_n = layer_norm(mem, mem_ln_g, mem_ln_b)
    for l in range(DEPTH):
        mix = mixer_sublayer(x, w_in[l], b_in[l], conv_a_w[l], conv_a_b[l], ln_a_g[l], ln_a_b[l],
                             w_a_out[l], b_a_out[l], conv_b_w[l], w_b_out[l], pool_w[l],
                             pool_scale[l], w_mix_out[l])
        x = layer_norm(DEEPNORM_ALPHA * x + mix, ln1_g[l], ln1_b[l])
        xa = memory_cross_attention(x, mem_n, w_xq[l], w_xk[l], w_xv[l], w_xo[l])
        x = layer_norm(DEEPNORM_ALPHA * x + xa, ln2_g[l], ln2_b[l])
        ff = moe_sublayer(x, router_w[l], router_b[l], w_gu[l], b_gu[l], w_down[l], b_down[l])
        x = layer_norm(DEEPNORM_ALPHA * x + ff, ln3_g[l], ln3_b[l])
    return x


DEPTH_2 = 2

HEAD_DIM = 64
N_SB_HEADS = 8
N_MOBA_HEADS = 8
N_ATT_HEADS = N_SB_HEADS + N_MOBA_HEADS
ATT_W = N_ATT_HEADS * HEAD_DIM
SB_QBLOCK = 128
MOBA_BLOCK = 256
MOBA_TOPK = 3
MOBA_QBLOCK = 32
N_RET_HEADS = 4
RET_DK = D_MODEL // N_RET_HEADS
RET_DV = 2 * RET_DK
RET_QK_W = N_RET_HEADS * RET_DK
RET_V_W = N_RET_HEADS * RET_DV
RET_CHUNK = 128
D_FF = -(-8 * D_MODEL // 768) * 256
ROPE_THETA = 10000.0
NORM_EPS = 1e-6
GN_EPS = 1e-5
NEG = -1e30
N_EVEN = (DEPTH_2 + 1) // 2
N_ODD = DEPTH_2 // 2


def rms_norm(x, g):
    xf = x.astype(jnp.float32)
    y = xf * lax.rsqrt(jnp.mean(xf * xf, axis=-1, keepdims=True) + NORM_EPS)
    return (y * g.astype(jnp.float32)).astype(x.dtype)

def rotary(x, pos):
    d = x.shape[-1]
    inv = ROPE_THETA ** (-jnp.arange(0, d, 2, dtype=jnp.float32) / d)
    ang = pos.astype(jnp.float32)[:, None] * inv[None, :]
    cos, sin = jnp.cos(ang), jnp.sin(ang)
    xf = x.astype(jnp.float32)
    x1, x2 = xf[..., : d // 2], xf[..., d // 2:]
    out = jnp.concatenate([x1 * cos - x2 * sin, x2 * cos + x1 * sin], axis=-1)
    return out.astype(x.dtype)

def ada_mod(c, w, b):
    m = jax.nn.silu(c) @ w + b
    return jnp.split(m[:, None, :], 6, axis=-1)

def modulate(h, shift, scale):
    return h * (1 + scale) + shift

def stick_breaking_attention(q, k, v):
    B, H, S, D = q.shape
    nblk = S // SB_QBLOCK
    kpos = jnp.arange(S)
    scale = D ** -0.5

    def block(i):
        start = i * SB_QBLOCK
        qb = lax.dynamic_slice_in_dim(q, start, SB_QBLOCK, axis=2)
        z = jnp.einsum('bhqd,bhkd->bhqk', qb, k).astype(jnp.float32) * scale
        qpos = start + jnp.arange(SB_QBLOCK)
        strict = kpos[None, :] < qpos[:, None]
        log_1mb = jnp.where(strict, jax.nn.log_sigmoid(-z), 0.0)
        after = lax.cumsum(log_1mb, axis=3, reverse=True) - log_1mb
        a = jnp.where(strict, jnp.exp(jax.nn.log_sigmoid(z) + after), 0.0)
        return jnp.einsum('bhqk,bhkd->bhqd', a.astype(v.dtype), v)

    out = lax.map(block, jnp.arange(nblk))
    return jnp.moveaxis(out, 0, 2).reshape(B, H, S, D)

def moba_attention(q, k, v):
    B, H, S, D = q.shape
    nb = -(-S // MOBA_BLOCK)
    spad = nb * MOBA_BLOCK
    pad = ((0, 0), (0, 0), (0, spad - S), (0, 0))
    kp = jnp.pad(k, pad)
    vp = jnp.pad(v, pad)
    kb = kp.reshape(B, H, nb, MOBA_BLOCK, D)
    vb = vp.reshape(B, H, nb, MOBA_BLOCK, D)
    kmean = jnp.mean(kb.astype(jnp.float32), axis=3).astype(k.dtype)
    kk = min(MOBA_TOPK, nb)
    scale = D ** -0.5
    nqb = S // MOBA_QBLOCK
    bi = jnp.arange(B)[:, None, None, None]
    hi = jnp.arange(H)[None, :, None, None]
    blk_ids = jnp.arange(nb)
    kpos_in = jnp.arange(MOBA_BLOCK)

    def block(i):
        start = i * MOBA_QBLOCK
        qb = lax.dynamic_slice_in_dim(q, start, MOBA_QBLOCK, axis=2)
        qpos = start + jnp.arange(MOBA_QBLOCK)
        own = start // MOBA_BLOCK
        gate = jnp.einsum('bhqd,bhnd->bhqn', qb, kmean).astype(jnp.float32)
        gate = jnp.where(blk_ids < own, gate, NEG)
        _, idx = lax.top_k(gate, kk)
        sel_valid = idx < own
        ksel = kb[bi, hi, idx]
        vsel = vb[bi, hi, idx]
        s_past = jnp.einsum('bhqd,bhqnkd->bhqnk', qb, ksel).astype(jnp.float32) * scale
        s_past = jnp.where(sel_valid[..., None], s_past, NEG)
        s_past = s_past.reshape(B, H, MOBA_QBLOCK, kk * MOBA_BLOCK)
        k_own = lax.dynamic_slice_in_dim(kp, own * MOBA_BLOCK, MOBA_BLOCK, axis=2)
        v_own = lax.dynamic_slice_in_dim(vp, own * MOBA_BLOCK, MOBA_BLOCK, axis=2)
        s_own = jnp.einsum('bhqd,bhkd->bhqk', qb, k_own).astype(jnp.float32) * scale
        kpos_own = own * MOBA_BLOCK + kpos_in
        s_own = jnp.where(kpos_own[None, :] <= qpos[:, None], s_own, NEG)
        p = jax.nn.softmax(jnp.concatenate([s_past, s_own], axis=-1), axis=-1).astype(v.dtype)
        p_past = p[..., : kk * MOBA_BLOCK].reshape(B, H, MOBA_QBLOCK, kk, MOBA_BLOCK)
        p_own = p[..., kk * MOBA_BLOCK:]
        return (jnp.einsum('bhqnk,bhqnkd->bhqd', p_past, vsel)
                + jnp.einsum('bhqk,bhkd->bhqd', p_own, v_own))

    out = lax.map(block, jnp.arange(nqb))
    return jnp.moveaxis(out, 0, 2).reshape(B, H, S, D)

def retention_chunkwise(q, k, v):
    B, H, S, dk = q.shape
    dv = v.shape[-1]
    C = RET_CHUNK
    nc = S // C
    log_g = jnp.log(1.0 - 2.0 ** (-5.0 - jnp.arange(H, dtype=jnp.float32)))
    n = jnp.arange(C, dtype=jnp.float32)
    diff = n[:, None] - n[None, :]
    decay = jnp.where(diff >= 0, jnp.exp(log_g[:, None, None] * jnp.maximum(diff, 0.0)), 0.0)
    xi = jnp.exp(log_g[:, None] * (n + 1.0))
    zeta = jnp.exp(log_g[:, None] * (C - 1.0 - n))
    chunk_decay = jnp.exp(log_g * C)

    def chunks(t):
        return jnp.moveaxis(t.reshape(B, H, nc, C, t.shape[-1]), 2, 0)

    def step(state, inp):
        qi, ki, vi = inp
        inner = jnp.einsum('bhqd,bhkd->bhqk', qi, ki).astype(jnp.float32) * decay
        o = (jnp.einsum('bhqk,bhkv->bhqv', inner, vi.astype(jnp.float32))
             + jnp.einsum('bhqd,bhdv->bhqv', qi.astype(jnp.float32), state) * xi[..., None])
        state = state * chunk_decay[:, None, None] + jnp.einsum(
            'bhkd,bhkv->bhdv', ki.astype(jnp.float32) * zeta[..., None], vi.astype(jnp.float32))
        return state, o

    init = jnp.zeros((B, H, dk, dv), jnp.float32)
    _, out = lax.scan(step, init, (chunks(q), chunks(k), chunks(v)))
    return jnp.moveaxis(out, 0, 2).reshape(B, H, S, dv)

def attn_hybrid_mixer(h, w_qkv, w_o, pos):
    B, S, _ = h.shape
    qkv = (h @ w_qkv).reshape(B, S, 3, N_ATT_HEADS, HEAD_DIM).transpose(2, 0, 3, 1, 4)
    q, k, v = qkv[0], qkv[1], qkv[2]
    sb = stick_breaking_attention(q[:, :N_SB_HEADS], k[:, :N_SB_HEADS], v[:, :N_SB_HEADS])
    qm = rotary(q[:, N_SB_HEADS:], pos)
    km = rotary(k[:, N_SB_HEADS:], pos)
    mb = moba_attention(qm, km, v[:, N_SB_HEADS:])
    o = jnp.concatenate([sb, mb], axis=1).transpose(0, 2, 1, 3).reshape(B, S, ATT_W)
    return o @ w_o

def retention_mixer(h, w_in, gn_gain, w_o, pos):
    B, S, _ = h.shape
    proj = h @ w_in
    q, k, v, g = jnp.split(proj, [RET_QK_W, 2 * RET_QK_W, 2 * RET_QK_W + RET_V_W], axis=-1)

    def heads(t, d):
        return t.reshape(B, S, N_RET_HEADS, d).transpose(0, 2, 1, 3)

    q = rotary(heads(q, RET_DK), pos)
    k = rotary(heads(k, RET_DK), pos) * (RET_DK ** -0.5)
    v = heads(v, RET_DV)
    o = retention_chunkwise(q, k, v)
    mu = jnp.mean(o, axis=-1, keepdims=True)
    var = jnp.mean(jnp.square(o - mu), axis=-1, keepdims=True)
    o = (o - mu) * lax.rsqrt(var + GN_EPS)
    o = o.transpose(0, 2, 1, 3).reshape(B, S, RET_V_W) * gn_gain.astype(jnp.float32)
    return (jax.nn.silu(g) * o.astype(h.dtype)) @ w_o

def swiglu(h, w_gate_up, w_down):
    gt, up = jnp.split(h @ w_gate_up, 2, axis=-1)
    return (jax.nn.silu(gt) * up) @ w_down

def second_inputs(seed: int = 0) -> dict:
    key = jax.random.key(seed)
    ks = jax.random.split(key, 14)
    f32 = jnp.float32

    def nrm(k, shape, fan_in):
        return jax.random.normal(k, shape, f32) * (fan_in ** -0.5)

    return {
        "x": jax.random.normal(ks[0], (BATCH, SEQ, D_MODEL), f32),
        "c": jax.random.normal(ks[1], (BATCH, D_MODEL), f32),
        "ada_w": nrm(ks[2], (DEPTH_2, D_MODEL, 6 * D_MODEL), D_MODEL),
        "ada_b": 0.02 * jax.random.normal(ks[3], (DEPTH_2, 6 * D_MODEL), f32),
        "norm_gains": 1.0 + 0.05 * jax.random.normal(ks[4], (DEPTH_2, 2, D_MODEL), f32),
        "att_w_qkv": nrm(ks[5], (N_EVEN, D_MODEL, 3 * ATT_W), D_MODEL),
        "att_w_o": nrm(ks[6], (N_EVEN, ATT_W, D_MODEL), ATT_W),
        "ret_w_in": nrm(ks[7], (N_ODD, D_MODEL, 2 * RET_QK_W + 2 * RET_V_W), D_MODEL),
        "ret_gn": 1.0 + 0.05 * jax.random.normal(ks[8], (N_ODD, RET_V_W), f32),
        "ret_w_o": nrm(ks[9], (N_ODD, RET_V_W, D_MODEL), RET_V_W),
        "ffn_w_gate_up": nrm(ks[10], (DEPTH_2, D_MODEL, 2 * D_FF), D_MODEL),
        "ffn_w_down": nrm(ks[11], (DEPTH_2, D_FF, D_MODEL), D_FF),
        "final_norm": 1.0 + 0.05 * jax.random.normal(ks[12], (D_MODEL,), f32),
    }

def second_block(x, c, ada_w, ada_b, norm_gains, att_w_qkv, att_w_o, ret_w_in, ret_gn,
              ret_w_o, ffn_w_gate_up, ffn_w_down, final_norm):
    S = x.shape[1]
    pos = jnp.arange(S, dtype=jnp.int32)
    for layer in range(DEPTH_2):
        shift_m, scale_m, gate_m, shift_f, scale_f, gate_f = ada_mod(c, ada_w[layer], ada_b[layer])
        h = modulate(rms_norm(x, norm_gains[layer, 0]), shift_m, scale_m)
        j = layer // 2
        if layer % 2 == 0:
            y = attn_hybrid_mixer(h, att_w_qkv[j], att_w_o[j], pos)
        else:
            y = retention_mixer(h, ret_w_in[j], ret_gn[j], ret_w_o[j], pos)
        x = x + gate_m * y
        h = modulate(rms_norm(x, norm_gains[layer, 1]), shift_f, scale_f)
        x = x + gate_f * swiglu(h, ffn_w_gate_up[layer], ffn_w_down[layer])
    return rms_norm(x, final_norm)


def setup_inputs(seed=0):
    out = dict(first_inputs(seed))
    for name, value in second_inputs(seed + 1).items():
        if name != "x":
            out[name + "_2"] = value
    return out


def reference(
    x, mem, mem_ln_g, mem_ln_b, w_in, b_in, conv_a_w, conv_a_b, ln_a_g, ln_a_b, w_a_out,
    b_a_out, conv_b_w, w_b_out, pool_w, pool_scale, w_mix_out, ln1_g, ln1_b, w_xq, w_xk, w_xv,
    w_xo, ln2_g, ln2_b, router_w, router_b, w_gu, b_gu, w_down, b_down, ln3_g, ln3_b, c_2,
    ada_w_2, ada_b_2, norm_gains_2, att_w_qkv_2, att_w_o_2, ret_w_in_2, ret_gn_2, ret_w_o_2,
    ffn_w_gate_up_2, ffn_w_down_2, final_norm_2,
):
    x = first_block(
        x, mem, mem_ln_g, mem_ln_b, w_in, b_in, conv_a_w, conv_a_b, ln_a_g, ln_a_b, w_a_out,
        b_a_out, conv_b_w, w_b_out, pool_w, pool_scale, w_mix_out, ln1_g, ln1_b, w_xq, w_xk,
        w_xv, w_xo, ln2_g, ln2_b, router_w, router_b, w_gu, b_gu, w_down, b_down, ln3_g, ln3_b,
    )
    return second_block(
        x, c_2, ada_w_2, ada_b_2, norm_gains_2, att_w_qkv_2, att_w_o_2, ret_w_in_2, ret_gn_2,
        ret_w_o_2, ffn_w_gate_up_2, ffn_w_down_2, final_norm_2,
    )


_drawn_inputs = setup_inputs


def setup_inputs(seed=0):
    import zlib

    import numpy as np

    out = dict(_drawn_inputs(seed))
    spreads = {}
    factors = {'mem_ln_g': 4.962,
     'mem_ln_b': 2.891,
     'ln_a_b': 4.214,
     'b_a_out': 3.791,
     'b_gu': 8.0,
     'b_down': 8.0,
     'ret_gn_2': 2.883}
    for name, (base, spread) in spreads.items():
        noise = np.random.default_rng([zlib.crc32(name.encode()), seed]).standard_normal(out[name].shape)
        drawn = base * np.exp(spread * noise) if base else spread * noise
        out[name] = __import__('jax').numpy.asarray(drawn.astype(out[name].dtype))
    for name, factor in factors.items():
        out[name] = (out[name] * factor).astype(out[name].dtype)
    return out
```

```python
from contextlib import ExitStack

import concourse.bass as bass
import numpy as np
from concourse import mybir

F32 = mybir.dt.float32
I32 = mybir.dt.int32
U32 = mybir.dt.uint32
ALU = mybir.AluOpType
ACT = mybir.ActivationFunctionType
AX_X = mybir.AxisListType.X

P = 128
D = 1024
T = 256
DC = D // P
TT = T // P
COLS = 512
RING = 6
BANKS = 4
TAPS_A, TAPS_B = 31, 3
WINDOWS = (2, 4, 8, 16)
XHEADS, XD = 4, 256
NEXP, TOPK = 32, 4
CAP = 64
FAR = 1.0e6
LIMIT, SWISH = 7.0, 1.702
ALPHA = 2.0 ** 0.25
LN_EPS, RMS_EPS, GN_EPS = 1e-5, 1e-6, 1e-5
NEG = -1e30
FF = 2816
FC = FF // P
HD = 64
RH, RV = 4, 512

PARAMS = [("b_in", 72), ("conv_a_w", TAPS_A * DC), ("conv_b_w", TAPS_B * DC), ("mem_ln_g", DC), ("mem_ln_b", DC),
          ("conv_a_b", DC), ("ln_a_g", DC), ("ln_a_b", DC), ("b_a_out", DC), ("pool_scale", DC), ("ln1_g", DC),
          ("ln1_b", DC), ("ln2_g", DC), ("ln2_b", DC), ("ln3_g", DC), ("ln3_b", DC), ("c_2", DC),
          ("norm_gains_2", 4 * DC), ("ret_gn_2", 16), ("final_norm_2", DC), ("ada_b_2", 96), ("b_gu", NEXP * 16)]
PCOL, NPARAM = {}, 0
for _name, _n in PARAMS:
    PCOL[_name] = NPARAM
    NPARAM += _n

CONST1 = [("ident", P), ("later", P), ("before", P), ("slot", P), ("count", len(WINDOWS) * T), ("router_b", NEXP)]
CONST2 = [("ret_cos", T), ("ret_sin", T), ("rope_cos", T), ("rope_sin", T), ("swap", P), ("strict", P), ("causal", P)]
C1, NC1, C2, NC2 = {}, 0, {}, 0
for _name, _n in CONST1:
    C1[_name] = NC1
    NC1 += _n
for _name, _n in CONST2:
    C2[_name] = NC2
    NC2 += _n


class Tile:

    def __init__(self, parts):
        self.parts = parts
        self.freed = None


class Block:
    pass


class Plan:

    def __init__(self):
        self.tiles = []
        self.groups = 0
        self.loaded = [0] * RING

    def tile(self, parts):
        t = Tile(parts)
        t.n = len(self.tiles)
        t.slot = t.n % RING
        self.loaded[t.slot] += 16 * len(parts)
        t.loaded = self.loaded[t.slot]
        self.tiles.append(t)
        return t

    def block(self, parts, rows=D, groups=2):
        b = Block()
        b.tiles = []
        b.kc = rows // P
        for k0 in range(0, rows, D):
            k1 = min(k0 + D, rows)
            cut, at = [], 0
            for w, c0, n in parts:
                cut.append((w[k0:k1, c0:c0 + n], at, (k1 - k0) // P))
                at += n
            b.tiles.append(self.tile(cut))
        b.groups = list(range(self.groups, self.groups + groups))
        self.groups += groups
        for t in b.tiles:
            t.freed = ("mm_done", self.groups)
        return b


def build_program(nc, a, consts1, consts2, decay, params, out):
    with ExitStack() as ctx:
        def sb(name, shape, dt=F32):
            return ctx.enter_context(nc.sbuf_tensor(name, shape, dt))

        sems = {}

        def sem(name):
            if name not in sems:
                sems[name] = ctx.enter_context(nc.semaphore(name))
            return sems[name]

        bank = [ctx.enter_context(nc.psum_tensor(f"bank{i}", [P, 512], F32)) for i in range(8)]
        ring = [sb(f"ring{i}", [P, DC, COLS]) for i in range(RING)]
        arena = sb("arena", [P, 9 * DC * T])
        a_pad = sb("a_pad", [P, DC, T + TAPS_A - 1])
        cv_pad = sb("cv_pad", [P, DC, T + TAPS_B - 1])
        par = sb("par", [P, NPARAM])
        c1 = sb("c1", [P, NC1])
        ones = sb("ones", [P, P])
        mean_w = sb("mean_w", [P, P])
        mean_v = sb("mean_v", [P, P])
        eps = sb("eps", [P, 3])
        rstd = sb("rstd", [P, T])
        small = sb("small", [P, 64])
        silu_c = sb("silu_c", [P, DC])
        mod = sb("mod", [P, 96])
        gscale = sb("gscale", [P, 4 * DC])

        def big(i):
            return arena[:, i * DC * T:(i + 1) * DC * T].rearrange("p (c t) -> p c t", c=DC)

        def pc(name, i=0, n=1):
            return par[:, PCOL[name] + i:PCOL[name] + i + n]

        def k1(name, n=P):
            return c1[:, C1[name]:C1[name] + n]

        ident = k1("ident")
        xT, memT = big(0), big(1)
        conv, sq = big(2), big(3)
        gate_b, conv_b = big(4), big(5)
        pooled, m_sum = big(6), big(7)
        scratch = 8 * DC * T
        sg = [arena[:, scratch + 512 * i:scratch + 512 * (i + 1)] for i in range(2)]
        yb = [arena[:, scratch + 1024 + 512 * i:scratch + 1024 + 512 * (i + 1)] for i in range(2)]
        PADW = WINDOWS[-1]
        pool_in = arena[:, 7 * DC * T:7 * DC * T + DC * (T + PADW)].rearrange("p (c t) -> p c t", c=DC)
        win = [arena[:, scratch + 256 + i * 576:scratch + 256 + i * 576 + 2 * (T + PADW)].rearrange(
            "p (c t) -> p c t", c=2) for i in range(2)]
        resid = big(6)
        kT, v_tok = big(3), big(4).rearrange("p c t -> p (c t)").rearrange("p (m f) -> p m f", m=TT)
        qT, attn = big(2), big(5)

        plan = Plan()
        w_in = a["w_in"][0]
        O_SIG, O_GB, O_GC, O_V, O_POOL, O_G = D, 2 * D, 3 * D, 4 * D, 5 * D, 6 * D
        glu = [plan.block([(w_in, O_SIG + 256 * i, 256), (w_in, 256 * i, 256)]) for i in range(4)]
        cv = [plan.block([(w_in, O_GC + 256 * i, 256), (w_in, O_V + 256 * i, 256)]) for i in range(4)]
        gb = [plan.block([(w_in, O_GB + 512 * i, 512)]) for i in range(2)]
        pi = [plan.block([(w_in, O_POOL + 512 * i, 512)]) for i in range(2)]
        ada = []

        def ada_tiles(n):
            for _ in range(n):
                i = len(ada)
                t = plan.tile([(a["ada_w_2"][i // 12][:, (i % 12) * 512:(i % 12) * 512 + 512], 0, DC)])
                t.freed = ("ada_taken", i + 1)
                ada.append(t)


        branch_gate, branch_out = {}, {}
        pool_tile = None
        for name, off, w in (("c", 2 * D, None), ("b", D, "w_b_out"), ("a", 0, "w_a_out")):
            for i in range(2):
                branch_gate[name, i] = plan.block([(w_in, O_G + off + 512 * i, 512)])
                if w:
                    branch_out[name, i] = plan.block([(a[w][0], 512 * i, 512)])
                    ada_tiles(4)
                else:
                    if i == 0:
                        pool_tile = plan.tile([(None, 0, DC)])
                    branch_out[name, i] = Block()
                    branch_out[name, i].groups = [plan.groups, plan.groups + 1]
                    plan.groups += 2
                    pool_tile.freed = ("mm_done", plan.groups)
        mix = []
        for i in range(2):
            mix.append(plan.block([(a["w_mix_out"][0], 512 * i, 512)]))
            ada_tiles(4)
        xk = [plan.block([(a["w_xk"][0], 512 * i, 512)]) for i in range(2)]
        xv = [plan.block([(a["w_xv"][0], 512 * i, 512)]) for i in range(2)]
        xq = [plan.block([(a["w_xq"][0], 512 * i, 512)]) for i in range(2)]
        xo = [plan.block([(a["w_xo"][0], 512 * i, 512)]) for i in range(2)]
        N1 = len(plan.tiles)
        qkv_w, ret_w = a["att_w_qkv_2"][0], a["ret_w_in_2"][0]
        aq = [plan.block([(qkv_w, 512 * i, 512)]) for i in range(2)]
        ak = [plan.block([(qkv_w, D + 512 * i, 512)]) for i in range(2)]
        av = [plan.block([(qkv_w, 2 * D + 512 * i, 512)]) for i in range(2)]
        ao = [plan.block([(a["att_w_o_2"][0], 512 * i, 512)]) for i in range(2)]
        gate_up, down = [], []

        def plan_feed_forward(layer):
            w = a["ffn_w_gate_up_2"][layer]
            gate_up.append([plan.block([(w, 256 * i, 256), (w, FF + 256 * i, 256)]) for i in range(FC // 2)])
            down.append([plan.block([(a["ffn_w_down_2"][layer], 512 * i, 512)], rows=FF) for i in range(2)])

        plan_feed_forward(0)
        rq = [plan.block([(ret_w, 512 * i, 512)]) for i in range(2)]
        rk = [plan.block([(ret_w, D + 512 * i, 512)]) for i in range(2)]
        rv = [plan.block([(ret_w, 2 * D + 512 * i, 512)]) for i in range(4)]
        rg = [plan.block([(ret_w, 4 * D + 512 * i, 512)]) for i in range(4)]
        ro = [plan.block([(a["ret_w_o_2"][0], 512 * i, 512)], rows=2 * D) for i in range(2)]
        plan_feed_forward(1)

        loaded = [sem(f"loaded{i}") for i in range(RING)]
        evac = [sem(f"evacuated{i}") for i in range(BANKS)]
        mloaded = [sem(f"expert_loaded{i}") for i in range(RING)]

        def at(t):
            return ring[t.slot]

        def wait_evac(eng, g):
            eng.wait_ge(evac[g % BANKS], g // BANKS + 1)

        def wait_evac_all(eng, blocks):
            gs = [g for b in blocks for g in b.groups]
            for g in gs[-BANKS:]:
                wait_evac(eng, g)

        def half(b):
            return b.rearrange("p (c t) -> p c t", c=2)

        def row(t):
            return t.rearrange("p (o t) -> p o t", o=1).to_broadcast([P, DC, T])

        def cut(o, n):
            return arena[:, o:o + n]

        h_tok = big(1).rearrange("p c t -> p (c t)").rearrange("p (i f) -> p i f", i=TT)
        acc = big(2)
        e0 = 3 * DC * T
        xg_s, xgT = cut(e0, 512), cut(e0 + 512, 512).rearrange("p (h c j) -> p h c j", h=2, c=4)
        gu_s = [cut(e0 + 1024 + 512 * i, 512) for i in range(2)]
        gu_t = [cut(e0 + 2048 + 512 * i, 512) for i in range(2)]
        sig = [cut(e0 + 3072 + 256 * i, 256) for i in range(2)]
        actT = cut(e0 + 3584, 512).rearrange("p (c j) -> p c j", c=DC)
        y_s, GT = cut(e0 + 4096, 512), cut(e0 + 4608, 256)
        Ssel = [cut(e0 + 4864 + 64 * i, 64) for i in range(2)]
        Gsel = [cut(e0 + 4992 + 128 * i, 128) for i in range(2)]
        r0 = e0 + 5248
        rw = cut(r0, 256).rearrange("p (k e) -> p k e", k=DC)
        lgT, gateT = cut(r0 + 256, 256), cut(r0 + 512, 256)
        bdown = cut(r0 + 768, 1024)
        r1 = r0 + 1792

        def pair32(k):
            return cut(r1 + 64 * k, 64).rearrange("p (i e) -> p i e", i=2)

        lg, mask, ex, gates, posr = [pair32(k) for k in range(5)]
        top8 = cut(r1 + 320, 16).rearrange("p (i e) -> p i e", i=2)
        idxf = cut(r1 + 336, 16).rearrange("p (i e) -> p i e", i=2)
        negm, den, rden, cmax, over = (cut(r1 + 352 + 2 * k, 2) for k in range(5))
        idx = sb("idx", [P, 2, 8], U32)
        nrounds = sb("nrounds", [P, 1], I32)

        c2 = a_pad[:, :, :].rearrange("p c t -> p (c t)")
        att_a = [c2[:, NC2 + 384 * i:NC2 + 384 * (i + 1)] for i in range(2)]
        dec = cv_pad[:, :, :].rearrange("p c t -> p (c t)")[:, 0:RH * T].rearrange("p (h t) -> p h t", h=RH)

        def k2(name, n=P):
            return c2[:, C2[name]:C2[name] + n]

        prob = [cut(scratch + 512 * h, 512) for h in range(XHEADS)]
        pT = [cut(DC * T + 512 * h, 512) for h in range(XHEADS)]
        xmax, xneg, xsum, xrec = (small[:, 8 * k:8 * k + 8] for k in range(4))
        bmax, bneg, bsum, brec = (small[:, 32 + 4 * k:36 + 4 * k] for k in range(4))
        ada_acc = [a_pad[:, :, :].rearrange("p c t -> p (c t)")[:, 512 * i:512 * i + 512] for i in range(2)]
        NSB = 8
        attn2, q2, kk2 = big(1), big(3), big(4)
        v2 = big(5).rearrange("p c t -> p (c t)").rearrange("p (i f) -> p i f", i=TT)
        v2r = cut(5 * DC * T, 2 * DC * T).rearrange("p (i f) -> p i f", i=TT)
        hidden = cut(3 * DC * T, FC * T).rearrange("p (c t) -> p c t", c=FC)
        t0 = 7 * DC * T
        a_e, a_r, a_L, a_t, a_A = ([cut(t0 + 768 * k + 384 * i, 384) for i in range(2)] for k in range(5))
        rope_t = cut(t0, 512)
        ff_s = [cut(t0 + 512 * i, 512) for i in range(2)]
        ret_o = cut(DC * T, 2 * DC * T).rearrange("p (c t) -> p c t", c=16)
        ret_g = cut(7 * DC * T, 2 * DC * T).rearrange("p (c t) -> p c t", c=16)
        ret_sq = cut(3 * DC * T, 2 * DC * T).rearrange("p (c t) -> p c t", c=16)
        rot_t = [cut(DC * T + 1024 * i, 1024).rearrange("p (h t) -> p h t", h=RH) for i in range(2)]
        gn_std = cv_pad[:, :, :].rearrange("p c t -> p (c t)")[:, RH * T:2 * RH * T].rearrange("p (h t) -> p h t", h=RH)

        class Norm:
            count, centred = 0, 0

            def __init__(self, src, sq, dst, g, b, mean, eps_col, centre=True):
                self.src, self.sq, self.dst, self.g, self.b = src, sq, dst, g, b
                self.mean, self.eps = mean, eps[:, eps_col:eps_col + 1]
                self.n = Norm.count = Norm.count + 1
                if centre:
                    Norm.centred += 1
                self.c = Norm.centred if centre else None

        def cols(name):
            return lambda c: pc(name, c)

        n_mem = Norm(memT, sq, memT, cols("mem_ln_g"), cols("mem_ln_b"), mean_w, 0)
        n_conv = Norm(conv, sq, conv, cols("ln_a_g"), cols("ln_a_b"), mean_w, 0)
        n_1 = Norm(resid, big(5), xT, cols("ln1_g"), cols("ln1_b"), mean_w, 0)
        n_2 = Norm(resid, big(2), xT, cols("ln2_g"), cols("ln2_b"), mean_w, 0)
        n_3 = Norm(acc, big(1), xT, cols("ln3_g"), cols("ln3_b"), mean_w, 0)

        def mcol(layer, j):
            return lambda c: mod[:, 48 * layer + DC * j + c:48 * layer + DC * j + c + 1]

        def scol(k):
            return lambda c: gscale[:, DC * k + c:DC * k + c + 1]

        rms = [Norm(xT, big(1), big(2), scol(k), mcol(k // 2, 3 * (k % 2)), mean_w, 1, False) for k in range(4)]
        n_end = Norm(xT, big(1), big(2), cols("final_norm_2"), None, mean_w, 1, False)

        block = ctx.enter_context(nc.Block())

        @block.sync
        def _(sp):
            sp.dma_start(xT[:, 0:4, :], a["xT"][0:512, :].rearrange("(c p) t -> p c t", p=P)).then_inc(sem("x_in"), 16)
            sp.dma_start(xT[:, 4:8, :], a["xT"][512:D, :].rearrange("(c p) t -> p c t", p=P)).then_inc(sem("x_in"), 16)
            sp.dma_start(par[:, :], params).then_inc(sem("par_in"), 16)

            def load_tile(t):
                if t.n >= RING and not N1 <= t.n < N1 + RING:
                    name, value = plan.tiles[t.n - RING].freed
                    sp.wait_ge(sem(name), value)
                for w, at_col, kc in t.parts:
                    if w is None:
                        sp.dma_start(ring[t.slot][:, :, 0:256],
                                     a["pool_w"][0].rearrange("g (k p) n -> p (g k) n", p=P)).then_inc(loaded[t.slot], 16)
                    else:
                        sp.dma_start(ring[t.slot][:, 0:kc, at_col:at_col + w.shape[1]],
                                     w.rearrange("(k p) n -> p k n", p=P)).then_inc(loaded[t.slot], 16)

            for t in plan.tiles[:4]:
                load_tile(t)
            sp.dma_start(memT, a["memT"].rearrange("(c p) t -> p c t", p=P)).then_inc(sem("mem_in"), 16)
            sp.dma_start(c1[:, :], consts1).then_inc(sem("c1_in"), 16)
            for t in plan.tiles[4:N1]:
                load_tile(t)

            def expert_tile(e, k):
                if k < 4:
                    src = a["w_gu"][0][e, :, D * (k % 2) + 512 * (k // 2):D * (k % 2) + 512 * (k // 2) + 512]
                else:
                    src = a["w_down"][0][e, :, 512 * (k - 4):512 * (k - 4) + 512]
                sp.dma_start(ring[k][:, :, :], src.rearrange("(k p) n -> p k n", p=P)).then_inc(mloaded[k], 16)

            for k in range(RING):
                last = max(n for n in range(N1) if n % RING == k)
                name, value = plan.tiles[last].freed
                sp.wait_ge(sem(name), value)
                expert_tile(0, k)
            sp.wait_ge(sem("ln_out"), n_2.n)
            sp.dma_start(rw, a["router_w"][0].rearrange("(k p) e -> p k e", p=P)).then_inc(sem("router_in"), 16)
            sp.dma_start(bdown[0:NEXP, :], a["b_down"][0]).then_inc(sem("router_in"), 16)
            sp.dma_start(c2[:, 0:NC2], consts2).then_inc(sem("c2_in"), 16)
            sp.dma_start(dec, decay.rearrange("p (h t) -> p h t", h=RH)).then_inc(sem("c2_in"), 16)
            sp.wait_ge(sem("rounds_ready"), 1)
            n = sp.value_load(nrounds[0:1, 0:1], min_val=1, max_val=T // CAP)
            with sp.Fori(1, n * NEXP) as it:
                for k in range(RING):
                    if k % 2 == 0:
                        sp.wait_ge(sem(("m_gu0", "m_gu1", "m_down")[k // 2]), it)
                    expert_tile(it % NEXP, k)
            for t in plan.tiles[N1:]:
                if t.n < N1 + RING:
                    sp.wait_ge(sem(("m_gu0", "m_gu1", "m_down")[t.slot // 2]), n * NEXP)
                load_tile(t)
            sp.wait_ge(sem("ln_out"), n_end.n)
            sp.dma_start(out.rearrange("(c p) t -> p c t", p=P), n_end.dst).then_inc(sem("out_stored"), 16)
            sp.wait_ge(sem("out_stored"), 16)

        @block.tensor
        def _(pe):
            def open_group(g):
                if g >= BANKS:
                    pe.wait_ge(evac[g % BANKS], g // BANKS)
                return bank[g % BANKS]

            def arrived(t):
                pe.wait_ge(loaded[t.slot], t.loaded)

            def feature(b, rhs, one=None):
                for j, g in enumerate(b.groups):
                    if one is not None and j != one:
                        continue
                    acc_bank = open_group(g)
                    for ch in range(2):
                        for kc in range(b.kc):
                            t = b.tiles[kc // DC]
                            if j == 0 and ch == 0 and kc % DC == 0:
                                arrived(t)
                            col = (2 * j + ch) * P
                            mm = pe.matmul(acc_bank[:, ch * T:(ch + 1) * T], at(t)[:, kc % DC, col:col + P],
                                           rhs[:, kc, :], start=kc == 0, stop=kc == b.kc - 1)
                    mm.then_inc(sem("mm_done"), 1)

            def token(b, lhs):
                for j, g in enumerate(b.groups):
                    acc_bank = open_group(g)
                    if j == 0:
                        arrived(b.tiles[0])
                    for kc in range(DC):
                        mm = pe.matmul(acc_bank[:, :], lhs[:, kc, j * P:(j + 1) * P], at(b.tiles[0])[:, kc, :],
                                       start=kc == 0, stop=kc == DC - 1)
                    mm.then_inc(sem("mm_done"), 1)

            def norm_mean(n):
                for c in range(DC):
                    mm = pe.matmul(bank[4][:, 0:T], n.mean[:, :], n.src[:, c, :], start=c == 0, stop=c == DC - 1)
                mm.then_inc(sem("ln_mean"), 1)

            def norm_var(n):
                pe.wait_ge(sem("ln_sq"), n.n)
                for c in range(DC):
                    mm = pe.matmul(bank[5][:, 0:T], n.mean[:, :], n.sq[:, c, :], start=c == 0, stop=c == DC - 1)
                mm.then_inc(sem("ln_var"), 1)

            def ada_reduce(i):
                pe.wait_ge(sem("ada_taken"), i + 1)
                for q in range(4):
                    mm = pe.matmul(bank[7][:, 4 * i + q:4 * i + q + 1], ada_acc[i % 2][:, q * P:(q + 1) * P],
                                   ones[:, 0:1], start=True, stop=True)
                mm.then_inc(sem("ada_reduced"), 1)

            pe.wait_ge(sem("consts_set"), 3)
            pe.wait_ge(sem("x_in"), 32)
            for b in glu:
                feature(b, xT)
            pe.wait_ge(sem("mem_in"), 16)
            norm_mean(n_mem)
            for b in cv:
                feature(b, xT)
            norm_var(n_mem)
            for b in gb + pi:
                feature(b, xT)
            for i in range(2):
                feature(branch_gate["c", i], xT)
                if i == 0:
                    pe.wait_ge(sem("pooled_ready"), len(WINDOWS))
                    arrived(pool_tile)
                for j, g in enumerate(branch_out["c", i].groups):
                    acc_bank = open_group(g)
                    grp = 2 * i + j
                    for ch in range(2):
                        for kc in range(2):
                            mm = pe.matmul(acc_bank[:, ch * T:(ch + 1) * T],
                                           at(pool_tile)[:, 2 * grp + kc, ch * P:(ch + 1) * P],
                                           pooled[:, 2 * grp + kc, :], start=kc == 0, stop=kc == 1)
                    mm.then_inc(sem("mm_done"), 1)
            pe.wait_ge(sem("conv_step"), TAPS_A * DC)
            norm_mean(n_conv)
            feature(branch_gate["b", 0], xT)
            pe.wait_ge(sem("gated"), 1)
            feature(branch_out["b", 0], gate_b)
            norm_var(n_conv)
            for i in range(0, 3):
                ada_reduce(i)
            feature(branch_gate["b", 1], xT)
            feature(branch_out["b", 1], gate_b)
            for i in range(3, 7):
                ada_reduce(i)
            feature(branch_gate["a", 0], xT)
            pe.wait_ge(sem("silu_a"), 1)
            feature(branch_out["a", 0], conv)
            for i in range(7, 11):
                ada_reduce(i)
            feature(branch_gate["a", 1], xT)
            feature(branch_out["a", 1], conv)
            for i in range(11, 15):
                ada_reduce(i)
            pe.wait_ge(sem("mixed"), 12)
            feature(mix[0], m_sum)
            for i in range(15, 19):
                ada_reduce(i)
            feature(mix[1], m_sum)
            wait_evac_all(pe, mix)
            norm_mean(n_1)
            feature(xk[0], memT)
            norm_var(n_1)
            feature(xk[1], memT)
            for i in range(19, 24):
                ada_reduce(i)
            for b in xv:
                token(b, memT)
            pe.wait_ge(sem("ln_out"), n_1.n)
            for b in xq:
                feature(b, xT)
            wait_evac_all(pe, xk + xv + xq)
            pe.wait_ge(sem("mod_ready"), 1)
            for h in range(XHEADS):
                for i in range(TT):
                    for k in range(2):
                        mm = pe.matmul(bank[4 + h][:, i * T:(i + 1) * T], qT[:, 2 * h + k, i * P:(i + 1) * P],
                                       kT[:, 2 * h + k, :], start=k == 0, stop=k == 1)
                mm.then_inc(sem("x_scores"), 1)
            for h in range(XHEADS + 1):
                if h < XHEADS:
                    pe.wait_ge(sem("x_prob"), h + 1)
                    for j in range(TT):
                        for i in range(TT):
                            mm = pe.transpose(bank[4 + h][:, j * T + i * P:j * T + (i + 1) * P],
                                              half(prob[h])[:, i, j * P:(j + 1) * P], ident)
                    mm.then_inc(sem("x_turned"), 1)
                if h > 0:
                    pe.wait_ge(sem("x_pT"), h)
                    for c in range(2):
                        for j in range(TT):
                            f = XD * (h - 1) + P * c
                            mm = pe.matmul(bank[3 + h][:, c * T:(c + 1) * T], v_tok[:, j, f:f + P],
                                           half(pT[h - 1])[:, j, :], start=j == 0, stop=j == TT - 1)
                    mm.then_inc(sem("x_out"), 1)
            pe.wait_ge(sem("x_oT"), XHEADS)
            for b in xo:
                feature(b, attn)
            wait_evac_all(pe, xo)
            norm_mean(n_2)
            norm_var(n_2)
            pe.wait_ge(sem("ln_out"), n_2.n)

            pe.wait_ge(sem("router_in"), 32)
            for k in range(DC):
                mm = pe.matmul(bank[4][0:NEXP, 0:T], rw[:, k, :], xT[:, k, :], start=k == 0, stop=k == DC - 1)
            mm.then_inc(sem("r_logitsT"), 1)
            for q in range(4):
                for c in range(4):
                    i, f = q // 2, 4 * (q % 2) + c
                    mm = pe.transpose(bank[q][:, c * P:(c + 1) * P], xT[:, f, i * P:(i + 1) * P], ident)
                mm.then_inc(sem("r_tok"), 1)
            pe.wait_ge(sem("r_lgT"), 1)
            for i in range(TT):
                mm = pe.matmul(bank[5][:, i * NEXP:(i + 1) * NEXP], lgT[0:NEXP, i * P:(i + 1) * P],
                               ident[0:NEXP, 0:NEXP], start=True, stop=True)
            mm.then_inc(sem("r_logits"), 1)
            pe.wait_ge(sem("r_mask"), 1)
            pe.matmul(bank[6][:, 0:NEXP], k1("before"), mask[:, 0, :], start=True, stop=True)
            pe.matmul(bank[6][:, NEXP:2 * NEXP], ones[:, :], mask[:, 0, :], start=True, stop=False)
            pe.matmul(bank[6][:, NEXP:2 * NEXP], k1("before"), mask[:, 1, :], start=False, stop=True)
            pe.matmul(bank[6][:, 2 * NEXP:3 * NEXP], ones[:, :], mask[:, 0, :], start=True, stop=False)
            pe.matmul(bank[6][:, 2 * NEXP:3 * NEXP], ones[:, :], mask[:, 1, :], start=False,
                      stop=True).then_inc(sem("r_pos"), 1)
            pe.wait_ge(sem("r_gates"), 1)
            for i in range(TT):
                mm = pe.matmul(bank[7][0:NEXP, i * P:(i + 1) * P], gates[:, i, :], ident, start=True, stop=True)
            mm.then_inc(sem("r_gateT"), 1)
            pe.wait_ge(sem("r_gateT_in"), 1)
            pe.wait_ge(sem("r_tok_in"), 4)
            for q in range(4):
                for ch in range(2):
                    c = 2 * q + ch
                    mm = pe.matmul(bank[q][:, ch * T:(ch + 1) * T], bdown[0:NEXP, c * P:(c + 1) * P],
                                   gateT[0:NEXP, :], start=True, stop=True)
                mm.then_inc(sem("r_bias"), 1)
            pe.wait_ge(sem("m_acc"), 4)
            pe.wait_ge(sem("rounds_ready"), 1)
            n = pe.value_load(nrounds[0:1, 0:1], min_val=1, max_val=T // CAP)
            with pe.Fori(0, n * NEXP) as it:
                def expert_loaded(k):
                    pe.wait_ge(mloaded[k], (it + 1) * 16)

                pe.wait_ge(sem("m_sel"), it + 1)
                pe.wait_ge(sem("m_acc"), it * 4 + 4)
                for i in range(TT):
                    for o in range(2):
                        pe.matmul(bank[4][64 * o:64 * o + 64, :], Ssel[i], h_tok[:, i, 512 * o:512 * o + 512],
                                  start=i == 0, stop=i == TT - 1)
                for i in range(TT):
                    mm = pe.transpose(bank[5][:, i * P:(i + 1) * P], Gsel[i], ident)
                mm.then_inc(sem("m_gather"), 1)
                pe.wait_ge(sem("m_xg"), it + 1)
                for c in range(4):
                    mm = pe.transpose(bank[6][:, c * P:(c + 1) * P], xg_s[:, c * P:(c + 1) * P], ident)
                mm.then_inc(sem("m_xturn"), 1)
                pe.wait_ge(sem("m_xgT"), it + 1)
                for b in range(2):
                    expert_loaded(2 * b)
                    expert_loaded(2 * b + 1)
                    for k in range(DC):
                        for o in range(2):
                            mm = pe.matmul(bank[b][64 * o:64 * o + 64, :], xgT[:, k // 4, k % 4, :],
                                           ring[2 * b + o][:, k, :], start=k == 0, stop=k == DC - 1)
                    mm.then_inc(sem(f"m_gu{b}"), 1)
                for b in range(2):
                    pe.wait_ge(sem("m_gus"), it * 2 + (b + 1))
                    for c in range(4):
                        mm = pe.transpose(bank[2 + b][:, c * P:(c + 1) * P], gu_s[b][:, c * P:(c + 1) * P], ident)
                    mm.then_inc(sem("m_guturn"), 1)
                expert_loaded(4)
                expert_loaded(5)
                for k in range(DC):
                    if k % 4 == 0:
                        pe.wait_ge(sem("m_act"), it * 2 + (k // 4 + 1))
                    for o in range(2):
                        mm = pe.matmul(bank[7][64 * o:64 * o + 64, :], actT[:, k, :], ring[4 + o][:, k, :],
                                       start=k == 0, stop=k == DC - 1)
                mm.then_inc(sem("m_down"), 1)
                pe.wait_ge(sem("m_ys"), it + 1)
                for q in range(4):
                    for ch in range(2):
                        c = 2 * q + ch
                        o = 64 * (c // 4)
                        mm = pe.matmul(bank[4 + q][:, ch * T:(ch + 1) * T], y_s[o:o + 64, (c % 4) * P:(c % 4 + 1) * P],
                                       GT[o:o + 64, :], start=True, stop=True)
                    mm.then_inc(sem("m_scatter"), 1)
            pe.wait_ge(sem("m_acc"), n * (4 * NEXP) + 4)
            norm_mean(n_3)
            norm_var(n_3)

            def rms_norm(n):
                pe.wait_ge(sem("ln_out"), n.n - 1)
                norm_var(n)
                pe.wait_ge(sem("ln_out"), n.n)

            def causal_out(dst, v_cols, probs, n_rows=P):
                pe.matmul(dst[:, 0:T], v_cols(0), probs[:, 0:T], start=True, stop=False)
                return pe.matmul(dst[:, P:T], v_cols(1), probs[:, T:T + P], start=False, stop=True)

            rms_norm(rms[0])
            for b in aq + ak:
                feature(b, rms[0].dst)
            for b in av:
                token(b, rms[0].dst)
            pe.wait_ge(sem("c2_in"), 32)
            wait_evac_all(pe, ak)
            for n_, X in enumerate((q2, kk2)):
                for p_ in range(2):
                    for ch in range(2):
                        mm = pe.matmul(bank[4 + 2 * n_ + p_][:, ch * T:(ch + 1) * T], k2("swap"),
                                       X[:, 4 + 2 * p_ + ch, :], start=True, stop=True)
                    mm.then_inc(sem("rope_mm"), 1)
            wait_evac_all(pe, av)
            pe.wait_ge(sem("roped"), 4)

            def head_rows(h):
                return slice(HD * (h % 2), HD * (h % 2) + HD), h // 2

            for i in range(NSB + 2):
                if i < NSB:
                    r, c = head_rows(i)
                    if i >= 2:
                        pe.wait_ge(sem("a_L"), i - 1)
                    b = bank[4 + i % 2]
                    pe.matmul(b[:, 0:T], kk2[r, c, 0:P], q2[r, c, :], start=True, stop=True)
                    pe.matmul(b[:, T:T + P], kk2[r, c, P:T], q2[r, c, P:T], start=True,
                              stop=True).then_inc(sem("a_z"), 1)
                if 1 <= i <= NSB:
                    h = i - 1
                    pe.wait_ge(sem("a_L"), h + 1)
                    if h >= 1:
                        pe.wait_ge(sem("a_t"), h)
                    L = a_L[h % 2]
                    pe.matmul(bank[6][:, 0:T], k1("later"), L[:, 0:T], start=True, stop=False)
                    pe.matmul(bank[6][:, P:T], ones[:, :], L[:, T:T + P], start=False, stop=True)
                    pe.matmul(bank[6][:, T:T + P], k1("later"), L[:, T:T + P], start=True,
                              stop=True).then_inc(sem("a_after"), 1)
                if i >= 2:
                    h = i - 2
                    r, c = head_rows(h)
                    pe.wait_ge(sem("a_A"), h + 1)
                    if h % 2 == 0 and h >= 2:
                        pe.wait_ge(sem("a_oT"), h // 2)
                    causal_out(bank[7][r, :], lambda j: v2[:, j, HD * h:HD * h + HD], a_A[h % 2]).then_inc(sem("a_o"), 1)
            pe.wait_ge(sem("a_oT"), NSB // 2)
            for i in range(NSB + 2):
                if i < NSB:
                    r, c = head_rows(NSB + i)
                    if i >= 2:
                        pe.wait_ge(sem("b_max"), i - 1)
                    b = bank[4 + i % 2]
                    pe.matmul(b[:, 0:P], q2[r, c, 0:P], kk2[r, c, 0:P], start=True, stop=True)
                    pe.matmul(b[:, P:P + T], q2[r, c, P:T], kk2[r, c, :], start=True,
                              stop=True).then_inc(sem("b_s"), 1)
                if 1 <= i <= NSB:
                    h = i - 1
                    pe.wait_ge(sem("b_prob"), h + 1)
                    if h >= 1:
                        pe.wait_ge(sem("b_pT"), h)
                    pr = a_t[h % 2]
                    pe.transpose(bank[6][:, 0:P], pr[:, 0:P], ident)
                    pe.transpose(bank[6][:, P:T], pr[:, P:T], ident)
                    pe.transpose(bank[6][:, T:T + P], pr[:, T:T + P], ident).then_inc(sem("b_turned"), 1)
                if i >= 2:
                    h = i - 2
                    r, c = head_rows(h)
                    pe.wait_ge(sem("b_pT"), h + 1)
                    if h % 2 == 0 and h >= 2:
                        pe.wait_ge(sem("b_oT"), h // 2)
                    causal_out(bank[7][r, :], lambda j: v2[:, j, HD * (NSB + h):HD * (NSB + h) + HD],
                               a_A[h % 2]).then_inc(sem("b_o"), 1)
            pe.wait_ge(sem("b_oT"), NSB // 2)
            for b in ao:
                feature(b, attn2)
            wait_evac_all(pe, ao)

            def feed_forward(layer):
                norm_var(rms[2 * layer + 1])
                pe.wait_ge(sem("ln_out"), rms[2 * layer + 1].n)
                for b in gate_up[layer]:
                    feature(b, rms[2 * layer + 1].dst)
                pe.wait_ge(sem("ff_hidden"), (layer + 1) * FC // 2)
                for b in down[layer]:
                    feature(b, hidden)
                wait_evac_all(pe, down[layer])

            feed_forward(0)
            norm_var(rms[2])
            pe.wait_ge(sem("ln_out"), rms[2].n)
            for b in rq + rk:
                feature(b, rms[2].dst)
            for b in rv:
                token(b, rms[2].dst)
            for b in rg:
                feature(b, rms[2].dst)
            pe.wait_ge(sem("ret_rot"), 2)
            wait_evac_all(pe, rv + rg)
            for i in range(RH + 1):
                if i < RH:
                    b = bank[4 + i % 2]
                    if i >= 2:
                        pe.wait_ge(sem("ret_inner"), i - 1)
                    for k in range(2):
                        pe.matmul(b[:, 0:T], kk2[:, 2 * i + k, 0:P], q2[:, 2 * i + k, :], start=k == 0, stop=k == 1)
                    for k in range(2):
                        mm = pe.matmul(b[:, T:T + P], kk2[:, 2 * i + k, P:T], q2[:, 2 * i + k, P:T], start=k == 0,
                                       stop=k == 1)
                    mm.then_inc(sem("ret_s"), 1)
                if i >= 1:
                    h = i - 1
                    pe.wait_ge(sem("ret_inner"), h + 1)
                    for cp in range(2):
                        n_ = 2 * h + cp
                        if n_ >= 2:
                            pe.wait_ge(sem("ret_o"), n_ - 1)
                        for ch in range(2):
                            f = RV * h + P * (2 * cp + ch)
                            mm = causal_out(bank[6 + n_ % 2][:, ch * T:(ch + 1) * T],
                                            lambda j: v2r[:, j, f:f + P], att_a[h % 2])
                        mm.then_inc(sem("ret_omm"), 1)
            pe.wait_ge(sem("ret_o"), 2 * RH)
            for src, done, need in ((ret_o, "gn_mean", None), (ret_sq, "gn_var", "gn_sq")):
                for h in range(RH):
                    b = bank[(4 if done == "gn_mean" else 6) + h // 2]
                    if need:
                        pe.wait_ge(sem(need), h + 1)
                    for c in range(4):
                        mm = pe.matmul(b[:, (h % 2) * T:(h % 2 + 1) * T], mean_v[:, :], src[:, 4 * h + c, :],
                                       start=c == 0, stop=c == 3)
                    if h % 2:
                        mm.then_inc(sem(done), 1)
            pe.wait_ge(sem("gn_out"), 1)
            for b in ro:
                feature(b, ret_o)
            wait_evac_all(pe, ro)
            feed_forward(1)
            norm_var(n_end)

        @block.scalar
        def _(act):
            steps = [0]

            def link(ins):
                steps[0] += 1
                ins.then_inc(sem("act_step"), 1)
                act.wait_ge(sem("act_step"), steps[0])

            def group(g, op):
                act.wait_ge(sem("mm_done"), g + 1)
                for ch in range(2):
                    ins = op(ch, bank[g % BANKS][:, ch * T:(ch + 1) * T])
                ins.then_inc(evac[g % BANKS], 1)

            def copy_group(g, dst):
                act.wait_ge(sem("mm_done"), g + 1)
                nc.scalar.activation(dst, bank[g % BANKS][:, :], ACT.Copy).then_inc(evac[g % BANKS], 1)

            def copy_features(blocks, dst):
                for i, b in enumerate(blocks):
                    for j, g in enumerate(b.groups):
                        copy_group(g, dst[:, 4 * i + 2 * j:4 * i + 2 * j + 2, :].rearrange("p c t -> p (c t)"))

            def copy_tokens(blocks, dst):
                for i, b in enumerate(blocks):
                    for j, g in enumerate(b.groups):
                        copy_group(g, dst[:, j, 512 * i:512 * i + 512])

            def norm_square(n):
                if n.c:
                    act.wait_ge(sem("ln_cen"), n.c)
                nc.scalar.activation(n.sq, n.src, ACT.Square).then_inc(sem("ln_sq"), 1)

            def norm_std(n):
                act.wait_ge(sem("ln_var"), n.n)
                if n.n > 1:
                    act.wait_ge(sem("ln_out"), n.n - 1)
                nc.scalar.activation(rstd[:, :], bank[5][:, 0:T], ACT.Sqrt, bias=n.eps).then_inc(sem("ln_std"), 1)

            act.wait_ge(sem("consts_set"), 3)
            act.wait_ge(sem("par_in"), 16)
            nc.scalar.activation(silu_c[:, :], pc("c_2", 0, DC), ACT.Silu).then_inc(sem("silu_c"), 1)
            for i, b in enumerate(glu):
                if i >= 2:
                    wait_evac(act, glu[i - 2].groups[1])
                group(b.groups[0], lambda ch, ps: nc.scalar.activation(
                    sg[i % 2][:, ch * T:(ch + 1) * T], ps, ACT.Sigmoid, bias=pc("b_in", O_SIG // P + 2 * i + ch)))
            norm_square(n_mem)
            for i, b in enumerate(cv):
                if i < 2:
                    wait_evac(act, glu[i + 2].groups[1])
                else:
                    act.wait_ge(sem("cv_ready"), i - 1)
                group(b.groups[0], lambda ch, ps: nc.scalar.activation(
                    sg[i % 2][:, ch * T:(ch + 1) * T], ps, ACT.Identity, bias=pc("b_in", O_GC // P + 2 * i + ch)))
                group(b.groups[1], lambda ch, ps: nc.scalar.activation(
                    yb[i % 2][:, ch * T:(ch + 1) * T], ps, ACT.Identity, bias=pc("b_in", O_V // P + 2 * i + ch)))
            norm_std(n_mem)
            for i, b in enumerate(gb):
                for j, g in enumerate(b.groups):
                    group(g, lambda ch, ps: nc.scalar.activation(
                        gate_b[:, 4 * i + 2 * j + ch, :], ps, ACT.Identity,
                        bias=pc("b_in", O_GB // P + 4 * i + 2 * j + ch)))
            act.wait_ge(sem("cv_ready"), 4)
            for i, b in enumerate(pi):
                for j, g in enumerate(b.groups):
                    group(g, lambda ch, ps: nc.scalar.activation(
                        pool_in[:, 4 * i + 2 * j + ch, PADW:], ps, ACT.Identity,
                        bias=pc("b_in", O_POOL // P + 4 * i + 2 * j + ch)))
            act.wait_ge(sem("pooled_ready"), len(WINDOWS))

            def branch(name, k, i, off, out_op):
                for j, g in enumerate(branch_gate[name, i].groups):
                    n = 4 * k + 2 * i + j
                    if n >= 2:
                        act.wait_ge(sem("mixed"), n - 1)
                    group(g, lambda ch, ps: nc.scalar.activation(
                        sg[n % 2][:, ch * T:(ch + 1) * T], ps, ACT.Sigmoid,
                        bias=pc("b_in", (O_G + off) // P + 4 * i + 2 * j + ch)))
                for j, g in enumerate(branch_out[name, i].groups):
                    n = 4 * k + 2 * i + j
                    group(g, lambda ch, ps: out_op(yb[n % 2][:, ch * T:(ch + 1) * T], ps, 4 * i + 2 * j + ch))

            for i in range(2):
                branch("c", 0, i, 2 * D, lambda o, ps, c: nc.scalar.activation(
                    o, ps, ACT.Copy, scale=pc("pool_scale", c)))
            norm_square(n_conv)
            branch("b", 1, 0, D, lambda o, ps, c: nc.scalar.activation(o, ps, ACT.Copy))
            norm_std(n_conv)
            branch("b", 1, 1, D, lambda o, ps, c: nc.scalar.activation(o, ps, ACT.Copy))
            act.wait_ge(sem("ln_out"), n_conv.n)
            for c in range(DC):
                ins = nc.scalar.activation(conv[:, c, :], conv[:, c, :], ACT.Silu, bias=n_conv.b(c), scale=n_conv.g(c))
            ins.then_inc(sem("silu_a"), 1)
            for i in range(2):
                branch("a", 2, i, 0, lambda o, ps, c: nc.scalar.activation(
                    o, ps, ACT.Identity, bias=pc("b_a_out", c)))
            norm_square(n_1)
            copy_features(xk[:1], kT)
            norm_std(n_1)
            copy_features(xk[1:], kT[:, 4:8, :])
            copy_tokens(xv, v_tok)
            copy_features(xq, qT)
            for h in range(XHEADS):
                act.wait_ge(sem("x_max"), h + 1)
                for i in range(TT):
                    ins = nc.scalar.activation(half(prob[h])[:, i, :], bank[4 + h][:, i * T:(i + 1) * T], ACT.Exp,
                                               bias=xneg[:, 2 * h + i:2 * h + i + 1], scale=XD ** -0.5,
                                               accum_out=xsum[:, 2 * h + i:2 * h + i + 1])
                ins.then_inc(sem("x_exp"), 1)
            for h in range(XHEADS + 1):
                if h < XHEADS:
                    act.wait_ge(sem("x_turned"), h + 1)
                    nc.scalar.activation(pT[h], bank[4 + h][:, :], ACT.Copy).then_inc(sem("x_pT"), 1)
                if h > 0:
                    act.wait_ge(sem("x_out"), h)
                    nc.scalar.activation(attn[:, 2 * h - 2:2 * h, :].rearrange("p c t -> p (c t)"), bank[3 + h][:, :],
                                         ACT.Copy).then_inc(sem("x_oT"), 1)
            norm_square(n_2)
            norm_std(n_2)
            act.wait_ge(sem("r_logitsT"), 1)
            nc.scalar.activation(lgT[0:NEXP, :], bank[4][0:NEXP, 0:T], ACT.Copy).then_inc(sem("r_lgT"), 1)
            for q in range(4):
                act.wait_ge(sem("r_tok"), q + 1)
                nc.scalar.activation(h_tok[:, q // 2, 512 * (q % 2):512 * (q % 2) + 512], bank[q][:, :],
                                     ACT.Copy).then_inc(sem("r_tok_in"), 1)
            act.wait_ge(sem("r_top"), 1)
            for i in range(TT):
                ins = nc.scalar.activation(ex[:, i, :], lg[:, i, :], ACT.Exp, bias=negm[:, i:i + 1])
            ins.then_inc(sem("r_exp"), 1)
            act.wait_ge(sem("r_gateT"), 1)
            nc.scalar.activation(gateT[0:NEXP, :], bank[7][0:NEXP, 0:T], ACT.Copy).then_inc(sem("r_gateT_in"), 1)
            act.wait_ge(sem("rounds_ready"), 1)
            n = act.value_load(nrounds[0:1, 0:1], min_val=1, max_val=T // CAP)
            with act.Fori(0, n * NEXP) as it:
                act.wait_ge(sem("m_gather"), it + 1)
                nc.scalar.activation(xg_s, bank[4][:, :], ACT.Copy).then_inc(sem("m_xg"), 1)
                nc.scalar.activation(GT, bank[5][:, 0:T], ACT.Copy)
                act.wait_ge(sem("m_xturn"), it + 1)
                nc.scalar.activation(xgT.rearrange("p h c j -> p c h j"),
                                     bank[6][:, :].rearrange("p (c h j) -> p c h j", c=4, h=2),
                                     ACT.Copy).then_inc(sem("m_xgT"), 1)
                for b in range(2):
                    act.wait_ge(sem(f"m_gu{b}"), it + 1)
                    nc.scalar.activation(gu_s[b], bank[b][:, :], ACT.Copy).then_inc(sem("m_gus"), 1)
                for b in range(2):
                    act.wait_ge(sem("m_gate"), it * 2 + (b + 1))
                    nc.scalar.activation(sig[b].rearrange("p (c j) -> p c j", c=4),
                                         gu_t[b].rearrange("p (c g j) -> p c g j", c=4, g=2)[:, :, 0, :],
                                         ACT.Sigmoid, scale=SWISH).then_inc(sem("m_sig"), 1)
                act.wait_ge(sem("m_down"), it + 1)
                nc.scalar.activation(y_s, bank[7][:, :], ACT.Copy).then_inc(sem("m_ys"), 1)
            norm_square(n_3)
            norm_std(n_3)

            def rms_norm(n):
                act.wait_ge(sem("ln_out"), n.n - 1)
                norm_square(n)
                norm_std(n)

            rms_norm(rms[0])
            copy_features(aq, q2)
            copy_features(ak, kk2)
            copy_tokens(av, v2)
            act.wait_ge(sem("roped"), 4)
            for i in range(NSB + 1):
                if i < NSB:
                    act.wait_ge(sem("a_z"), i + 1)
                    if i >= 2:
                        act.wait_ge(sem("a_L"), i - 1)
                    z = bank[4 + i % 2][:, 0:384]
                    link(nc.scalar.activation(a_e[i % 2], z, ACT.Abs))
                    link(nc.scalar.activation(a_e[i % 2], a_e[i % 2], ACT.Exp, scale=-HD ** -0.5))
                    link(nc.scalar.activation(a_e[i % 2], a_e[i % 2], ACT.Ln, bias=1.0))
                    nc.scalar.activation(a_r[i % 2], z, ACT.Relu, scale=HD ** -0.5).then_inc(sem("a_sp"), 1)
                if i >= 1:
                    h = i - 1
                    act.wait_ge(sem("a_t"), h + 1)
                    if h >= 2:
                        act.wait_ge(sem("a_o"), h - 1)
                    nc.scalar.activation(a_A[h % 2], a_t[h % 2], ACT.Exp).then_inc(sem("a_exp"), 1)
            act.wait_ge(sem("a_oT"), NSB // 2)
            for i in range(NSB + 1):
                if i < NSB:
                    act.wait_ge(sem("b_max"), i + 1)
                    k = i % 2
                    nc.scalar.activation(a_t[k][:, 0:P], a_L[k][:, 0:P], ACT.Exp, bias=bneg[:, 2 * k:2 * k + 1],
                                         accum_out=bsum[:, 2 * k:2 * k + 1])
                    nc.scalar.activation(a_t[k][:, P:P + T], a_L[k][:, P:P + T], ACT.Exp,
                                         bias=bneg[:, 2 * k + 1:2 * k + 2],
                                         accum_out=bsum[:, 2 * k + 1:2 * k + 2]).then_inc(sem("b_exp"), 1)
                if i >= 1:
                    h = i - 1
                    act.wait_ge(sem("b_turned"), h + 1)
                    if h >= 2:
                        act.wait_ge(sem("b_o"), h - 1)
                    nc.scalar.activation(a_A[h % 2], bank[6][:, 0:384], ACT.Copy).then_inc(sem("b_pT"), 1)

            def feed_forward(layer):
                norm_square(rms[2 * layer + 1])
                norm_std(rms[2 * layer + 1])
                for i, b in enumerate(gate_up[layer]):
                    m = layer * (FC // 2) + i
                    if i >= 2:
                        act.wait_ge(sem("ff_hidden"), m - 1)
                    g = b.groups[0]
                    act.wait_ge(sem("mm_done"), g + 1)
                    nc.scalar.activation(ff_s[i % 2], bank[g % BANKS][:, :], ACT.Silu).then_inc(evac[g % BANKS], 1)

            wait_evac_all(act, ao)
            feed_forward(0)
            wait_evac_all(act, down[0])
            norm_square(rms[2])
            norm_std(rms[2])
            copy_features(rq, q2)
            copy_features(rk, kk2)
            copy_tokens(rv, v2r)
            for i, b in enumerate(rg):
                for j, g in enumerate(b.groups):
                    act.wait_ge(sem("mm_done"), g + 1)
                    c = 4 * i + 2 * j
                    nc.scalar.activation(ret_g[:, c:c + 2, :].rearrange("p c t -> p (c t)"), bank[g % BANKS][:, :],
                                         ACT.Silu).then_inc(evac[g % BANKS], 1)
            for n_ in range(2 * RH):
                act.wait_ge(sem("ret_omm"), n_ + 1)
                if n_ == 0:
                    act.wait_ge(sem("ret_rot"), 2)
                nc.scalar.activation(ret_o[:, 2 * n_:2 * n_ + 2, :].rearrange("p c t -> p (c t)"),
                                     bank[6 + n_ % 2][:, :], ACT.Copy).then_inc(sem("ret_o"), 1)
            for h in range(RH):
                act.wait_ge(sem("gn_cen"), h + 1)
                nc.scalar.activation(ret_sq[:, 4 * h:4 * h + 4, :], ret_o[:, 4 * h:4 * h + 4, :],
                                     ACT.Square).then_inc(sem("gn_sq"), 1)
            for hp in range(2):
                act.wait_ge(sem("gn_var"), hp + 1)
                nc.scalar.activation(gn_std[:, 2 * hp:2 * hp + 2, :].rearrange("p c t -> p (c t)"), bank[6 + hp][:, :],
                                     ACT.Sqrt, bias=eps[:, 2:3]).then_inc(sem("gn_std"), 1)
            wait_evac_all(act, ro)
            feed_forward(1)
            wait_evac_all(act, down[1])
            norm_square(n_end)
            norm_std(n_end)

        @block.vector
        def _(dve):
            steps = [0]

            def link(ins):
                steps[0] += 1
                ins.then_inc(sem("dve_step"), 1)
                dve.wait_ge(sem("dve_step"), steps[0])

            V = nc.vector

            def bcast(b, n):
                return b.rearrange("p (o t) -> p o t", o=1).to_broadcast([P, n, T])

            def norm_centre(n):
                dve.wait_ge(sem("ln_mean"), n.c)
                V.tensor_tensor(n.src, n.src, bcast(bank[4][:, 0:T], DC), ALU.subtract).then_inc(sem("ln_cen"), 1)
                dve.wait_ge(sem("ln_cen"), n.c)

            def norm_finish(n, affine=True):
                dve.wait_ge(sem("ln_std"), n.n)
                link(V.reciprocal(rstd[:, :], rstd[:, :]))
                mid = n.src if n.c else n.dst
                if not affine:
                    V.tensor_tensor(mid, n.src, bcast(rstd[:, :], DC), ALU.mult).then_inc(sem("ln_out"), 1)
                    dve.wait_ge(sem("ln_out"), n.n)
                    return
                link(V.tensor_tensor(mid, n.src, bcast(rstd[:, :], DC), ALU.mult))
                for c in range(DC):
                    if n.b:
                        ins = V.tensor_scalar(n.dst[:, c, :], mid[:, c, :], n.g(c), n.b(c), ALU.mult, ALU.add)
                    else:
                        ins = V.tensor_scalar(n.dst[:, c, :], mid[:, c, :], n.g(c), None, ALU.mult)
                ins.then_inc(sem("ln_out"), 1)
                dve.wait_ge(sem("ln_out"), n.n)

            def ada_tile(i):
                t = ada[i]
                dve.wait_ge(loaded[t.slot], t.loaded)
                if i >= 2:
                    dve.wait_ge(sem("ada_reduced"), i - 1)
                o = ada_acc[i % 2]
                link(V.tensor_scalar(o, at(t)[:, 0, :], silu_c[:, 0:1], None, ALU.mult))
                for k in range(1, DC):
                    ins = V.scalar_tensor_tensor(out=o, in0=at(t)[:, k, :], scalar=silu_c[:, k:k + 1], in1=o,
                                                 op0=ALU.mult, op1=ALU.add)
                    if k < DC - 1:
                        link(ins)
                ins.then_inc(sem("ada_taken"), 1)
                dve.wait_ge(sem("ada_taken"), i + 1)

            def add_residual(blocks):
                for b, i in blocks:
                    for j, g in enumerate(b.groups):
                        dve.wait_ge(sem("mm_done"), g + 1)
                        c = 4 * i + 2 * j
                        V.scalar_tensor_tensor(out=resid[:, c:c + 2, :], in0=xT[:, c:c + 2, :], scalar=ALPHA,
                                               in1=half(bank[g % BANKS][:, :]), op0=ALU.mult,
                                               op1=ALU.add).then_inc(evac[g % BANKS], 1)

            V.memset(ones[:, :], 1.0).then_inc(sem("consts_set"), 1)
            V.memset(mean_w[:, :], 1.0 / D)
            V.memset(mean_v[:, :], 1.0 / RV).then_inc(sem("consts_set"), 1)
            V.memset(eps[:, 0:1], LN_EPS)
            V.memset(eps[:, 1:2], RMS_EPS)
            V.memset(eps[:, 2:3], GN_EPS).then_inc(sem("consts_set"), 1)
            dve.wait_ge(sem("par_in"), 16)
            for i, b in enumerate(glu):
                g = b.groups[1]
                wait_evac(dve, b.groups[0])
                dve.wait_ge(sem("mm_done"), g + 1)
                for ch in range(2):
                    ins = V.scalar_tensor_tensor(out=a_pad[:, 2 * i + ch, TAPS_A - 1:],
                                                 in0=bank[g % BANKS][:, ch * T:(ch + 1) * T],
                                                 scalar=pc("b_in", 2 * i + ch),
                                                 in1=sg[i % 2][:, ch * T:(ch + 1) * T], op0=ALU.add, op1=ALU.mult)
                ins.then_inc(evac[g % BANKS], 1)
            norm_centre(n_mem)
            dve.wait_ge(sem("pads_zero"), 2)
            wait_evac_all(dve, glu)
            for c in range(DC):
                V.tensor_scalar(conv[:, c, :], a_pad[:, c, 0:T], pc("conv_a_w", c), pc("conv_a_b", c), ALU.mult,
                                ALU.add).then_inc(sem("conv_step"), 1)
            with dve.Fori(1, TAPS_A) as tap:
                for c in range(DC):
                    dve.wait_ge(sem("conv_step"), tap * DC + (c + 1 - DC))
                    V.scalar_tensor_tensor(out=conv[:, c, :], in0=a_pad[:, c, bass.ds(tap, T)],
                                           scalar=par[:, bass.ds(tap * DC + (PCOL["conv_a_w"] + c), 1)],
                                           in1=conv[:, c, :], op0=ALU.mult, op1=ALU.add).then_inc(sem("conv_step"), 1)
            dve.wait_ge(sem("cv_ready"), 4)
            for tap in range(TAPS_B):
                for c in range(DC):
                    if tap == 0:
                        V.tensor_scalar(conv_b[:, c, :], cv_pad[:, c, 0:T], pc("conv_b_w", c), None,
                                        ALU.mult).then_inc(sem("cvb_step"), 1)
                        continue
                    dve.wait_ge(sem("cvb_step"), DC * (tap - 1) + c + 1)
                    V.scalar_tensor_tensor(out=conv_b[:, c, :], in0=cv_pad[:, c, tap:tap + T],
                                           scalar=pc("conv_b_w", tap * DC + c), in1=conv_b[:, c, :], op0=ALU.mult,
                                           op1=ALU.add).then_inc(sem("cvb_step"), 1)
            dve.wait_ge(sem("conv_step"), TAPS_A * DC)
            norm_centre(n_conv)
            dve.wait_ge(sem("silu_c"), 1)
            for i in range(0, 4):
                ada_tile(i)
            norm_finish(n_mem)
            norm_finish(n_conv, affine=False)
            for i in range(4, 16):
                ada_tile(i)
            add_residual([(mix[0], 0)])
            for i in range(16, 20):
                ada_tile(i)
            add_residual([(mix[1], 1)])
            norm_centre(n_1)
            for i in range(20, 22):
                ada_tile(i)
            norm_finish(n_1)
            for i in range(22, 24):
                ada_tile(i)
            dve.wait_ge(sem("ada_reduced"), 24)
            link(V.tensor_tensor(mod[:, :], bank[7][:, 0:96], pc("ada_b_2", 0, 96), ALU.add))
            for k in range(4):
                layer, j = k // 2, 1 + 3 * (k % 2)
                ins = V.scalar_tensor_tensor(out=gscale[:, DC * k:DC * (k + 1)],
                                             in0=mod[:, 48 * layer + DC * j:48 * layer + DC * (j + 1)], scalar=1.0,
                                             in1=pc("norm_gains_2", DC * k, DC), op0=ALU.add, op1=ALU.mult)
            ins.then_inc(sem("mod_ready"), 1)
            for h in range(XHEADS):
                dve.wait_ge(sem("x_scores"), h + 1)
                link(V.tensor_reduce(xmax[:, 2 * h:2 * h + 2], half(bank[4 + h][:, :]), AX_X, ALU.max))
                V.tensor_scalar(xneg[:, 2 * h:2 * h + 2], xmax[:, 2 * h:2 * h + 2], -XD ** -0.5, None,
                                ALU.mult).then_inc(sem("x_max"), 1)
            for h in range(XHEADS):
                dve.wait_ge(sem("x_exp"), h + 1)
                link(V.reciprocal(xrec[:, 2 * h:2 * h + 2], xsum[:, 2 * h:2 * h + 2]))
                for i in range(TT):
                    ins = V.tensor_scalar(half(prob[h])[:, i, :], half(prob[h])[:, i, :],
                                          xrec[:, 2 * h + i:2 * h + i + 1], None, ALU.mult)
                ins.then_inc(sem("x_prob"), 1)
            add_residual([(xo[0], 0), (xo[1], 1)])
            norm_centre(n_2)
            norm_finish(n_2)

            dve.wait_ge(sem("r_logits"), 1)
            dve.wait_ge(sem("c1_in"), 16)
            link(V.tensor_tensor(lg, bank[5][:, 0:2 * NEXP].rearrange("p (i e) -> p i e", i=2),
                                 k1("router_b", NEXP).rearrange("p (o e) -> p o e", o=1).to_broadcast([P, 2, NEXP]),
                                 ALU.add))
            for i in range(TT):
                ins = V.max(top8[:, i, :], lg[:, i, :])
            link(ins)
            for i in range(TT):
                V.max_index(idx[:, i, :], top8[:, i, :], lg[:, i, :])
            link(V.tensor_scalar(negm[:, 0:2], top8[:, :, 0:1].rearrange("p i e -> p (i e)"), -1.0, None, ALU.mult))
            link(V.tensor_copy(idxf, idx[:, :, :]))
            for k in range(TOPK):
                for i in range(TT):
                    if k == 0:
                        ins = V.tensor_scalar(mask[:, i, :], k1("slot", NEXP), idxf[:, i, 0:1], None, ALU.is_equal)
                    else:
                        ins = V.scalar_tensor_tensor(out=mask[:, i, :], in0=k1("slot", NEXP),
                                                     scalar=idxf[:, i, k:k + 1], in1=mask[:, i, :],
                                                     op0=ALU.is_equal, op1=ALU.add)
                if k < TOPK - 1:
                    link(ins)
            ins.then_inc(sem("r_mask"), 1)
            dve.wait_ge(sem("r_mask"), 1)
            dve.sem_inc(sem("r_top"), 1)
            dve.wait_ge(sem("r_exp"), 1)
            link(V.tensor_tensor(ex, ex, mask, ALU.mult))
            link(V.tensor_reduce(den[:, 0:2], ex, AX_X, ALU.add))
            link(V.reciprocal(rden[:, 0:2], den[:, 0:2]))
            for i in range(TT):
                ins = V.tensor_scalar(gates[:, i, :], ex[:, i, :], rden[:, i:i + 1], None, ALU.mult)
            ins.then_inc(sem("r_gates"), 1)
            dve.wait_ge(sem("r_gates"), 1)
            dve.wait_ge(sem("r_pos"), 1)
            link(V.tensor_reduce(cmax[:, 0:1], bank[6][:, 2 * NEXP:3 * NEXP], AX_X, ALU.max))
            link(V.tensor_scalar(over[:, 0:1], cmax[:, 0:1], float(CAP), 1.0, ALU.is_gt, ALU.add))
            for k in range(2, T // CAP):
                link(V.tensor_scalar(over[:, 1:2], cmax[:, 0:1], float(k * CAP), None, ALU.is_gt))
                link(V.tensor_tensor(over[:, 0:1], over[:, 0:1], over[:, 1:2], ALU.add))
            V.tensor_copy(nrounds[:, :], over[:, 0:1]).then_inc(sem("rounds_ready"), 1)
            link(V.scalar_tensor_tensor(out=posr, in0=bank[6][:, 0:2 * NEXP].rearrange("p (i e) -> p i e", i=2),
                                        scalar=-FAR, in1=mask, op0=ALU.add, op1=ALU.mult))
            link(V.tensor_scalar(posr, posr, FAR, None, ALU.add))
            for q in range(4):
                dve.wait_ge(sem("r_bias"), q + 1)
                V.scalar_tensor_tensor(out=acc[:, 2 * q:2 * q + 2, :], in0=xT[:, 2 * q:2 * q + 2, :], scalar=ALPHA,
                                       in1=half(bank[q][:, :]), op0=ALU.mult, op1=ALU.add).then_inc(sem("m_acc"), 1)
            dve.wait_ge(sem("m_acc"), 4)
            dve.wait_ge(sem("rounds_ready"), 1)
            n = dve.value_load(nrounds[0:1, 0:1], min_val=1, max_val=T // CAP)
            slot = k1("slot")
            with dve.Fori(0, n) as r:
                with dve.Fori(0, NEXP) as e:
                    it = r * NEXP + e
                    for i in range(TT):
                        V.tensor_scalar(Ssel[i], slot[:, 0:CAP], posr[:, i, bass.ds(e, 1)], None, ALU.is_equal)
                        ins = V.tensor_scalar(Gsel[i], slot, posr[:, i, bass.ds(e, 1)], gates[:, i, bass.ds(e, 1)],
                                              ALU.is_equal, ALU.mult)
                    ins.then_inc(sem("m_sel"), 1)
                    for b in range(2):
                        tv = gu_t[b].rearrange("p (c j) -> p c j", c=8)
                        gate = gu_t[b].rearrange("p (c g j) -> p c g j", c=4, g=2)[:, :, 0, :]
                        up = gu_t[b].rearrange("p (c g j) -> p c g j", c=4, g=2)[:, :, 1, :]
                        bias = par[:, bass.ds(e * 16 + (PCOL["b_gu"] + 8 * b), 8)].rearrange(
                            "p (c o) -> p c o", o=1).to_broadcast([P, 8, CAP])
                        dve.wait_ge(sem("m_guturn"), it * 2 + (b + 1))
                        V.tensor_tensor(tv, bank[2 + b][:, :].rearrange("p (c j) -> p c j", c=8), bias,
                                        ALU.add).then_inc(sem("m_vec"), 1)
                        dve.wait_ge(sem("m_vec"), it * 8 + (4 * b + 1))
                        V.tensor_scalar(gate, gate, LIMIT, None, ALU.min).then_inc(sem("m_gate"), 1)
                        V.tensor_scalar(up, up, LIMIT, -LIMIT, ALU.min, ALU.max).then_inc(sem("m_vec"), 1)
                        dve.wait_ge(sem("m_vec"), it * 8 + (4 * b + 2))
                        dve.wait_ge(sem("m_gate"), it * 2 + (b + 1))
                        V.scalar_tensor_tensor(out=up, in0=up, scalar=1.0, in1=gate, op0=ALU.add,
                                               op1=ALU.mult).then_inc(sem("m_vec"), 1)
                        dve.wait_ge(sem("m_vec"), it * 8 + (4 * b + 3))
                        dve.wait_ge(sem("m_sig"), it * 2 + (b + 1))
                        V.tensor_tensor(actT[:, 4 * b:4 * b + 4, :], up, sig[b].rearrange("p (c j) -> p c j", c=4),
                                        ALU.mult).then_inc(sem("m_act"), 1)
                        dve.sem_inc(sem("m_vec"), 1)
                    for q in range(4):
                        dve.wait_ge(sem("m_scatter"), it * 4 + (q + 1))
                        V.tensor_tensor(acc[:, 2 * q:2 * q + 2, :], acc[:, 2 * q:2 * q + 2, :],
                                        half(bank[4 + q][:, :]), ALU.add).then_inc(sem("m_acc"), 1)
                    dve.wait_ge(sem("m_acc"), it * 4 + 8)
                V.tensor_scalar(posr, posr, -float(CAP), None, ALU.add).then_inc(sem("m_round"), 1)
                dve.wait_ge(sem("m_round"), r + 1)
            norm_centre(n_3)
            norm_finish(n_3)

            dve.wait_ge(sem("mod_ready"), 1)
            norm_finish(rms[0])
            dve.wait_ge(sem("c2_in"), 32)
            for n_, (X, blocks) in enumerate(((q2, aq), (kk2, ak))):
                wait_evac_all(dve, blocks)
                for p_ in range(2):
                    c = 4 + 2 * p_
                    dve.wait_ge(sem("rope_mm"), 2 * n_ + p_ + 1)
                    link(V.tensor_tensor(half(rope_t), half(bank[4 + 2 * n_ + p_][:, :]), bcast(k2("rope_sin", T), 2),
                                         ALU.mult))
                    link(V.tensor_tensor(X[:, c:c + 2, :], X[:, c:c + 2, :], bcast(k2("rope_cos", T), 2), ALU.mult))
                    V.tensor_tensor(X[:, c:c + 2, :], X[:, c:c + 2, :], half(rope_t), ALU.add).then_inc(sem("roped"), 1)
                    dve.wait_ge(sem("roped"), 2 * n_ + p_ + 1)

            def diag(b):
                return b.rearrange("p (k j) -> p k j", k=3)[:, 0:3:2, :]

            def mask2(name):
                return k2(name).rearrange("p (o j) -> p o j", o=1).to_broadcast([P, 2, P])

            for i in range(NSB + 2):
                if i < NSB:
                    k = i % 2
                    dve.wait_ge(sem("a_sp"), i + 1)
                    if i >= 2:
                        dve.wait_ge(sem("a_after"), i - 1)
                        dve.wait_ge(sem("a_exp"), i - 1)
                    link(V.tensor_tensor(a_L[k], a_r[k], a_e[k], ALU.add))
                    link(V.scalar_tensor_tensor(out=a_t[k], in0=bank[4 + k][:, 0:384], scalar=HD ** -0.5, in1=a_L[k],
                                                op0=ALU.mult, op1=ALU.subtract))
                    V.tensor_tensor(diag(a_L[k]), diag(a_L[k]), mask2("strict"), ALU.mult).then_inc(sem("a_L"), 1)
                if 1 <= i <= NSB:
                    h = i - 1
                    k = h % 2
                    dve.wait_ge(sem("a_after"), h + 1)
                    V.tensor_tensor(a_t[k], a_t[k], bank[6][:, 0:384], ALU.subtract).then_inc(sem("a_t"), 1)
                    dve.wait_ge(sem("a_exp"), h + 1)
                    V.tensor_tensor(diag(a_A[k]), diag(a_A[k]), mask2("strict"), ALU.mult).then_inc(sem("a_A"), 1)
                if i >= 3 and i % 2:
                    h = i - 2
                    dve.wait_ge(sem("a_o"), h + 1)
                    V.tensor_copy(attn2[:, h // 2, :], bank[7][:, 0:T]).then_inc(sem("a_oT"), 1)
            dve.wait_ge(sem("a_A"), NSB)
            for i in range(NSB + 2):
                if i < NSB:
                    k = i % 2
                    dve.wait_ge(sem("b_s"), i + 1)
                    if i >= 2:
                        dve.wait_ge(sem("b_exp"), i - 1)
                    link(V.tensor_scalar(a_L[k], bank[4 + k][:, 0:384], HD ** -0.5, None, ALU.mult))
                    link(V.tensor_tensor(diag(a_L[k]), diag(a_L[k]), mask2("causal"), ALU.add))
                    V.tensor_reduce(bmax[:, 2 * k:2 * k + 1], a_L[k][:, 0:P], AX_X, ALU.max)
                    link(V.tensor_reduce(bmax[:, 2 * k + 1:2 * k + 2], a_L[k][:, P:P + T], AX_X, ALU.max))
                    V.tensor_scalar(bneg[:, 2 * k:2 * k + 2], bmax[:, 2 * k:2 * k + 2], -1.0, None,
                                    ALU.mult).then_inc(sem("b_max"), 1)
                if 1 <= i <= NSB:
                    h = i - 1
                    k = h % 2
                    dve.wait_ge(sem("b_exp"), h + 1)
                    link(V.reciprocal(brec[:, 2 * k:2 * k + 2], bsum[:, 2 * k:2 * k + 2]))
                    V.tensor_scalar(a_t[k][:, 0:P], a_t[k][:, 0:P], brec[:, 2 * k:2 * k + 1], None, ALU.mult)
                    V.tensor_scalar(a_t[k][:, P:P + T], a_t[k][:, P:P + T], brec[:, 2 * k + 1:2 * k + 2], None,
                                    ALU.mult).then_inc(sem("b_prob"), 1)
                if i >= 3 and i % 2:
                    h = i - 2
                    dve.wait_ge(sem("b_o"), h + 1)
                    V.tensor_copy(attn2[:, NSB // 2 + h // 2, :], bank[7][:, 0:T]).then_inc(sem("b_oT"), 1)

            def add_gated(blocks, gate):
                for i, b in enumerate(blocks):
                    for j, g in enumerate(b.groups):
                        dve.wait_ge(sem("mm_done"), g + 1)
                        for ch in range(2):
                            c = 4 * i + 2 * j + ch
                            ins = V.scalar_tensor_tensor(out=xT[:, c, :], in0=bank[g % BANKS][:, ch * T:(ch + 1) * T],
                                                         scalar=gate(c), in1=xT[:, c, :], op0=ALU.mult, op1=ALU.add)
                        ins.then_inc(evac[g % BANKS], 1)
                wait_evac_all(dve, blocks)

            def feed_forward(layer):
                norm_finish(rms[2 * layer + 1])
                for i, b in enumerate(gate_up[layer]):
                    g = b.groups[1]
                    wait_evac(dve, b.groups[0])
                    dve.wait_ge(sem("mm_done"), g + 1)
                    V.tensor_tensor(hidden[:, 2 * i:2 * i + 2, :], half(bank[g % BANKS][:, :]), half(ff_s[i % 2]),
                                    ALU.mult).then_inc(evac[g % BANKS], 1)
                    wait_evac(dve, g)
                    dve.sem_inc(sem("ff_hidden"), 1)
                add_gated(down[layer], mcol(layer, 5))

            add_gated(ao, mcol(0, 2))
            feed_forward(0)
            norm_finish(rms[2])
            for n_, (X, blocks) in enumerate(((q2, rq), (kk2, rk))):
                wait_evac_all(dve, blocks)
                hv = X.rearrange("p (h s) t -> p h s t", s=2)
                x1, x2 = hv[:, :, 0, :], hv[:, :, 1, :]
                cos, sin = bcast(k2("ret_cos", T), RH), bcast(k2("ret_sin", T), RH)
                link(V.tensor_tensor(rot_t[0], x2, sin, ALU.mult))
                link(V.tensor_tensor(rot_t[1], x1, sin, ALU.mult))
                link(V.tensor_tensor(x1, x1, cos, ALU.mult))
                link(V.tensor_tensor(x2, x2, cos, ALU.mult))
                link(V.tensor_tensor(x1, x1, rot_t[0], ALU.subtract))
                V.tensor_tensor(x2, x2, rot_t[1], ALU.add).then_inc(sem("ret_rot"), 1)
                dve.wait_ge(sem("ret_rot"), n_ + 1)
            for h in range(RH):
                k = h % 2
                dve.wait_ge(sem("ret_s"), h + 1)
                if h >= 2:
                    dve.wait_ge(sem("ret_omm"), 2 * (h - 1))
                V.tensor_tensor(att_a[k][:, 0:T], bank[4 + k][:, 0:T], dec[:, h, :], ALU.mult)
                V.tensor_tensor(att_a[k][:, T:T + P], bank[4 + k][:, T:T + P], dec[:, h, 0:P],
                                ALU.mult).then_inc(sem("ret_inner"), 1)
            for h in range(RH):
                dve.wait_ge(sem("gn_mean"), h // 2 + 1)
                oh = ret_o[:, 4 * h:4 * h + 4, :]
                V.tensor_tensor(oh, oh, bcast(bank[4 + h // 2][:, (h % 2) * T:(h % 2 + 1) * T], 4),
                                ALU.subtract).then_inc(sem("gn_cen"), 1)
            dve.wait_ge(sem("gn_cen"), RH)
            dve.wait_ge(sem("gn_std"), 2)
            link(V.reciprocal(gn_std, gn_std))
            for h in range(RH):
                oh = ret_o[:, 4 * h:4 * h + 4, :]
                ins = V.tensor_tensor(oh, oh, bcast(gn_std[:, h, :], 4), ALU.mult)
            link(ins)
            for c in range(16):
                ins = V.scalar_tensor_tensor(out=ret_o[:, c, :], in0=ret_o[:, c, :], scalar=pc("ret_gn_2", c),
                                             in1=ret_g[:, c, :], op0=ALU.mult, op1=ALU.mult)
            ins.then_inc(sem("gn_out"), 1)
            dve.wait_ge(sem("gn_out"), 1)
            add_gated(ro, mcol(1, 2))
            feed_forward(1)
            norm_finish(n_end)

        @block.gpsimd
        def _(pool):
            steps = [0]

            def link(ins):
                steps[0] += 1
                ins.then_inc(sem("pool_step"), 1)
                pool.wait_ge(sem("pool_step"), steps[0])

            G = nc.gpsimd
            G.memset(a_pad[:, :, 0:TAPS_A - 1], 0.0).then_inc(sem("pads_zero"), 1)
            G.memset(cv_pad[:, :, 0:TAPS_B - 1], 0.0).then_inc(sem("pads_zero"), 1)
            for i, b in enumerate(cv):
                wait_evac(pool, b.groups[0])
                wait_evac(pool, b.groups[1])
                G.tensor_tensor(cv_pad[:, 2 * i:2 * i + 2, TAPS_B - 1:], half(sg[i % 2]), half(yb[i % 2]),
                                ALU.mult).then_inc(sem("cv_ready"), 1)
            pool.wait_ge(sem("cv_ready"), 4)
            link(G.memset(pool_in[:, :, 0:PADW], 0.0))
            pool.wait_ge(sem("c1_in"), 16)
            wait_evac_all(pool, gb + pi)
            for k, w in enumerate(WINDOWS):
                u = pool_in[:, 2 * k:2 * k + 2, :]
                src, shift = u, 1
                while shift < w:
                    dst = win[(shift.bit_length() - 1) % 2]
                    first = 2 * shift - 1
                    link(G.tensor_tensor(dst[:, :, first:], src[:, :, first:], src[:, :, first - shift:T + PADW - shift],
                                         ALU.add))
                    src, shift = dst, 2 * shift
                count = c1[:, C1["count"] + k * T:C1["count"] + (k + 1) * T].rearrange(
                    "p (o t) -> p o t", o=1).to_broadcast([P, 2, T])
                link(G.tensor_tensor(pooled[:, 2 * k:2 * k + 2, :], src[:, :, PADW:], count, ALU.mult))
                G.tensor_tensor(pooled[:, 2 * k:2 * k + 2, :], pooled[:, 2 * k:2 * k + 2, :], u[:, :, PADW:],
                                ALU.subtract).then_inc(sem("pooled_ready"), 1)
                pool.wait_ge(sem("pooled_ready"), k + 1)

            def mix_in(name, k, i):
                for j in range(2):
                    n = 4 * k + 2 * i + j
                    wait_evac(pool, branch_gate[name, i].groups[j])
                    wait_evac(pool, branch_out[name, i].groups[j])
                    m = m_sum[:, 4 * i + 2 * j:4 * i + 2 * j + 2, :]
                    if k == 0:
                        G.tensor_tensor(m, half(sg[n % 2]), half(yb[n % 2]), ALU.mult).then_inc(sem("mixed"), 1)
                    else:
                        link(G.tensor_tensor(yb[n % 2], sg[n % 2], yb[n % 2], ALU.mult))
                        G.tensor_tensor(m, m, half(yb[n % 2]), ALU.add).then_inc(sem("mixed"), 1)
                    pool.wait_ge(sem("mixed"), n + 1)

            mix_in("c", 0, 0)
            mix_in("c", 0, 1)
            pool.wait_ge(sem("cvb_step"), TAPS_B * DC)
            G.tensor_tensor(gate_b, gate_b, conv_b, ALU.mult).then_inc(sem("gated"), 1)
            for k, name in ((1, "b"), (2, "a")):
                mix_in(name, k, 0)
                mix_in(name, k, 1)


def _columns(v):
    return np.ascontiguousarray(np.asarray(v).reshape(-1, P).T)


def _constants():
    i = np.arange(P)
    t = np.arange(T)
    one = {
        "ident": np.eye(P),
        "later": (i[:, None] > i[None, :]),
        "before": (i[:, None] < i[None, :]),
        "slot": np.tile(np.arange(CAP), (P, 2)),
        "count": np.tile(np.concatenate([1.0 / np.minimum(t + 1, w) for w in WINDOWS]), (P, 1)),
    }

    def angles(d, rows):
        inv = np.float32(10000.0) ** (-np.arange(0, d, 2, dtype=np.float32) / np.float32(d))
        return (t.astype(np.float32)[None, :] * inv[rows][:, None]).astype(np.float32)

    ret, rope = angles(XD, i), angles(HD, i % (HD // 2))
    swap = np.zeros((P, P))
    for m in range(P):
        if m % HD < HD // 2:
            swap[m + HD // 2, m] = -1.0
        else:
            swap[m - HD // 2, m] = 1.0
    two = {
        "ret_cos": np.cos(ret), "ret_sin": np.sin(ret), "rope_cos": np.cos(rope), "rope_sin": np.sin(rope),
        "swap": swap, "strict": (i[:, None] < i[None, :]), "causal": np.where(i[None, :] <= i[:, None], 0.0, NEG),
    }
    diff = t[None, :] - i[:, None]
    gamma = np.log(1.0 - 2.0 ** (-5.0 - np.arange(RH)))
    decay = [np.where(diff >= 0, np.exp(g * np.maximum(diff, 0)), 0.0) * XD ** -0.5 for g in gamma]
    return one, two, np.concatenate(decay, axis=1).astype(np.float32)


WEIGHTS = ["w_in", "w_a_out", "w_b_out", "pool_w", "w_mix_out", "w_xq", "w_xk", "w_xv", "w_xo", "router_w", "w_gu",
           "w_down", "b_down", "ada_w_2", "att_w_qkv_2", "att_w_o_2", "ret_w_in_2", "ret_w_o_2",
           "ffn_w_gate_up_2", "ffn_w_down_2"]


def kernel(**inputs):
    from concourse import bacc
    from concourse.bass_utils import run_bass_kernel_spmd

    arrays = {name: np.ascontiguousarray(inputs[name]) for name in WEIGHTS}
    arrays["xT"] = np.ascontiguousarray(np.asarray(inputs["x"])[0].T)
    arrays["memT"] = np.ascontiguousarray(np.asarray(inputs["mem"])[0].T)
    cols = {name: _columns(inputs[name]) for name, _ in PARAMS if name != "b_gu"}
    cols["b_gu"] = np.asarray(inputs["b_gu"])[0].reshape(NEXP, 2, 2, 4, P).transpose(4, 0, 2, 3, 1).reshape(P, -1)
    arrays["params"] = np.ascontiguousarray(np.concatenate([cols[name] for name, _ in PARAMS], axis=1))
    one, two, decay = _constants()
    one["router_b"] = np.repeat(np.asarray(inputs["router_b"]), P, axis=0)
    arrays["consts1"] = np.concatenate([one[name] for name, _ in CONST1], axis=1).astype(np.float32)
    arrays["consts2"] = np.concatenate([two[name] for name, _ in CONST2], axis=1).astype(np.float32)
    arrays["decay"] = decay

    nc = bacc.Bacc("TRN2", target_bir_lowering=False, num_devices=1)
    aps = {name: nc.dram_tensor(name, v.shape, mybir.dt.from_np(v.dtype), kind="ExternalInput").ap()
           for name, v in arrays.items()}
    out = nc.dram_tensor("outT", (D, T), F32, kind="ExternalOutput").ap()
    build_program(nc, aps, aps["consts1"], aps["consts2"], aps["decay"], aps["params"], out)
    r = run_bass_kernel_spmd(nc, [arrays], core_ids=[0])
    return np.ascontiguousarray(r.results[0]["outT"].T)[None]
```

```python
from contextlib import ExitStack

import concourse.bass as bass
import numpy as np
from concourse import mybir

F32 = mybir.dt.float32
F32R = mybir.dt.float32r
I32 = mybir.dt.int32
U32 = mybir.dt.uint32
ALU = mybir.AluOpType
ACT = mybir.ActivationFunctionType
AX_X = mybir.AxisListType.X

P = 128
D = 1024
T = 256
DC = D // P
TT = T // P
COLS = 512
RING = 4
HIGHS = 3
ERING = 6
HALF = COLS // 2
BANKS = 4
TAPS_A, TAPS_B = 31, 3
WINDOWS = (2, 4, 8, 16)
XHEADS, XD = 4, 256
NEXP, TOPK = 32, 4
CAP = 64
FAR = 1.0e6
LIMIT, SWISH = 7.0, 1.702
ALPHA = 2.0 ** 0.25
LN_EPS, RMS_EPS, GN_EPS = 1e-5, 1e-6, 1e-5
NEG = -1e30
FF = 2816
FC = FF // P
HD = 64
RH, RV = 4, 512

PARAMS = [("b_in", 72), ("conv_a_w", TAPS_A * DC), ("conv_b_w", TAPS_B * DC), ("mem_ln_g", DC), ("mem_ln_b", DC),
          ("conv_a_b", DC), ("ln_a_g", DC), ("ln_a_b", DC), ("b_a_out", DC), ("pool_scale", DC), ("ln1_g", DC),
          ("ln1_b", DC), ("ln2_g", DC), ("ln2_b", DC), ("ln3_g", DC), ("ln3_b", DC), ("c_2", DC),
          ("norm_gains_2", 4 * DC), ("ret_gn_2", 16), ("final_norm_2", DC), ("ada_b_2", 96), ("b_gu", NEXP * 16)]
PCOL, NPARAM = {}, 0
for _name, _n in PARAMS:
    PCOL[_name] = NPARAM
    NPARAM += _n

CONST1 = [("ident", P), ("later", P), ("before", P), ("slot", P), ("count", len(WINDOWS) * T), ("router_b", NEXP)]
CONST2 = [("ret_cos", T), ("ret_sin", T), ("rope_cos", T), ("rope_sin", T), ("swap", P), ("strict", P), ("causal", P)]
C1, NC1, C2, NC2 = {}, 0, {}, 0
for _name, _n in CONST1:
    C1[_name] = NC1
    NC1 += _n
for _name, _n in CONST2:
    C2[_name] = NC2
    NC2 += _n


class Tile:

    def __init__(self, parts):
        self.parts = parts
        self.freed = []


class Block:
    pass


class Unit:
    pass


class Plan:

    def __init__(self):
        self.tiles = []
        self.units = []
        self.groups = 0
        self.products = 0
        self.done = {}
        self.unit_of = {}
        self.loaded = [0] * RING
        self.lows = {"low_dve": 0, "low_pool": 0}

    def tile(self, parts):
        t = Tile(parts)
        t.n = len(self.tiles)
        t.slot = t.n % RING
        self.loaded[t.slot] += 16 * len(parts)
        t.loaded = self.loaded[t.slot]
        self.tiles.append(t)
        return t

    def block(self, parts, rows=D, low=("low_dve", "low_dve"), token=False):
        b = Block()
        b.kc = rows // P
        b.groups = [self.groups, self.groups + 1]
        self.groups += 2
        b.units = []
        for k0 in range(0, rows, D):
            k1 = min(k0 + D, rows)
            cut, at = [], 0
            for w, c0, n in parts:
                cut.append((w[k0:k1, c0:c0 + n], at, (k1 - k0) // P))
                at += n
            t = self.tile(cut)
            for j in range(2):
                u = Unit()
                u.n, u.tile, u.j, u.k0, u.kc, u.low = len(self.units), t, j, k0 // P, (k1 - k0) // P, low[j]
                self.lows[u.low] += 1
                u.low_n = self.lows[u.low]
                self.products += 1
                u.done = self.products
                self.units.append(u)
                b.units.append(u)
            t.freed = [("mm_done", self.products)]
        for j, g in enumerate(b.groups):
            last = b.units[-1] if token else b.units[-2 + j]
            self.done[g], self.unit_of[g] = last.done, last.n
        return b


def build_program(nc, a, consts1, consts2, decay, params, out):
    with ExitStack() as ctx:
        def sb(name, shape, dt=F32):
            return ctx.enter_context(nc.sbuf_tensor(name, shape, dt))

        sems = {}

        def sem(name):
            if name not in sems:
                sems[name] = ctx.enter_context(nc.semaphore(name))
            return sems[name]

        bank = [ctx.enter_context(nc.psum_tensor(f"bank{i}", [P, 512], F32)) for i in range(8)]
        ring = [sb(f"ring{i}", [P, DC, COLS]) for i in range(ERING)]
        slot_bytes = DC * COLS * 4
        ring_at = nc.sbuf_base - ERING * slot_bytes

        def alias(name, shape, offset):
            return nc.alloc_sbuf_tensor_at(name, shape, F32R, offset=offset)

        ring_low = [alias(f"ring_low{i}", [P, DC, COLS], ring_at + i * slot_bytes) for i in range(RING)]
        w_high = [alias(f"w_high{i}", [P, DC, HALF], ring_at + RING * slot_bytes + i * slot_bytes // 2) for i in range(2)]
        w_high.append(sb("w_high2", [P, DC, HALF], F32R))
        x_high, x_low = (alias(n, [P, DC, T], ring_at + (RING + 1) * slot_bytes + i * slot_bytes // 2)
                         for i, n in enumerate(("x_high", "x_low")))
        arena = sb("arena", [P, 9 * DC * T])
        arena_at = nc.sbuf_base - 9 * DC * T * 4
        arena_r = alias("arena_r", [P, 9 * DC * T], arena_at)
        a_pad = sb("a_pad", [P, DC, T + TAPS_A - 1])
        cv_pad = sb("cv_pad", [P, DC, T + TAPS_B - 1])
        par = sb("par", [P, NPARAM])
        c1 = sb("c1", [P, NC1])
        ones = sb("ones", [P, P])
        mean_w = sb("mean_w", [P, P])
        mean_v = sb("mean_v", [P, P])
        eps = sb("eps", [P, 3])
        rstd = sb("rstd", [P, T])
        small = sb("small", [P, 64])
        silu_c = sb("silu_c", [P, DC])
        mod = sb("mod", [P, 96])
        gscale = sb("gscale", [P, 4 * DC])

        ada_acc = [c1[:, C1["count"] + 512 * i:C1["count"] + 512 * (i + 1)] for i in range(2)]

        def big(i):
            return arena[:, i * DC * T:(i + 1) * DC * T].rearrange("p (c t) -> p c t", c=DC)

        def split_big(i, chunks=DC, at=0):
            o = i * DC * T + at
            return arena_r[:, o:o + chunks * T].rearrange("p (c t) -> p c t", c=chunks)

        def pc(name, i=0, n=1):
            return par[:, PCOL[name] + i:PCOL[name] + i + n]

        def k1(name, n=P):
            return c1[:, C1[name]:C1[name] + n]

        ident = k1("ident")
        xT, memT = big(0), big(1)
        conv, sq = big(2), big(3)
        gate_b, conv_b = big(4), big(5)
        pooled, m_sum = big(6), big(7)
        scratch = 8 * DC * T
        sg = [arena[:, scratch + 512 * i:scratch + 512 * (i + 1)] for i in range(2)]
        yb = [arena[:, scratch + 1024 + 512 * i:scratch + 1024 + 512 * (i + 1)] for i in range(2)]
        PADW = WINDOWS[-1]
        pool_in = arena[:, 7 * DC * T:7 * DC * T + DC * (T + PADW)].rearrange("p (c t) -> p c t", c=DC)
        win = [arena[:, scratch + 256 + i * 576:scratch + 256 + i * 576 + 2 * (T + PADW)].rearrange(
            "p (c t) -> p c t", c=2) for i in range(2)]
        resid = big(6)
        kT, v_tok = big(3), big(4).rearrange("p c t -> p (c t)").rearrange("p (m f) -> p m f", m=TT)
        qT, attn = big(2), big(5)

        plan = Plan()
        w_in = a["w_in"][0]
        O_SIG, O_GB, O_GC, O_V, O_POOL, O_G = D, 2 * D, 3 * D, 4 * D, 5 * D, 6 * D
        glu = [plan.block([(w_in, O_SIG + 256 * i, 256), (w_in, 256 * i, 256)]) for i in range(4)]
        gp = ("low_pool", "low_pool")
        both = ("low_pool", "low_dve")
        cv = [plan.block([(w_in, O_GC + 256 * i, 256), (w_in, O_V + 256 * i, 256)], low=gp) for i in range(4)]
        pi = [plan.block([(w_in, O_POOL + 512 * i, 512)], low=gp) for i in range(2)]
        gb = [plan.block([(w_in, O_GB + 512 * i, 512)], low=gp) for i in range(2)]
        ada = []

        def ada_tiles(n):
            for _ in range(n):
                i = len(ada)
                t = plan.tile([(a["ada_w_2"][i // 12][:, (i % 12) * 512:(i % 12) * 512 + 512], 0, DC)])
                t.freed = [("ada_taken", i + 1)]
                ada.append(t)


        branch_gate, branch_out = {}, {}
        pool_tile = None
        for name, off, w in (("c", 2 * D, None), ("b", D, "w_b_out"), ("a", 0, "w_a_out")):
            for i in range(2):
                branch_gate[name, i] = plan.block([(w_in, O_G + off + 512 * i, 512)], **({"low": both} if w else {}))
                if w:
                    ada_tiles(1)
                    branch_out[name, i] = plan.block([(a[w][0], 512 * i, 512)], low=both)
                    ada_tiles(1)
                else:
                    if i == 0:
                        pool_tile = plan.tile([(None, 0, DC)])
                    branch_out[name, i] = Block()
                    branch_out[name, i].groups = [plan.groups, plan.groups + 1]
                    for g in branch_out[name, i].groups:
                        plan.products += 1
                        plan.done[g] = plan.products
                    plan.groups += 2
                    pool_tile.freed = [("mm_done", plan.products)]
        mix = []
        for i in range(2):
            mix.append(plan.block([(a["w_mix_out"][0], 512 * i, 512)], low=both))
            ada_tiles(1)
        xk = []
        for i in range(2):
            xk.append(plan.block([(a["w_xk"][0], 512 * i, 512)], low=both))
            ada_tiles(1)
        xv = [plan.block([(a["w_xv"][0], 512 * i, 512)], low=both, token=True) for i in range(2)]
        xq = [plan.block([(a["w_xq"][0], 512 * i, 512)], low=both) for i in range(2)]
        xo = [plan.block([(a["w_xo"][0], 512 * i, 512)], low=both) for i in range(2)]
        N1, PRODUCTS1, UNITS1 = len(plan.tiles), plan.products, len(plan.units)
        qkv_w, ret_w = a["att_w_qkv_2"][0], a["ret_w_in_2"][0]
        aq = [plan.block([(qkv_w, 512 * i, 512)]) for i in range(2)]
        ak = [plan.block([(qkv_w, D + 512 * i, 512)]) for i in range(2)]
        av = [plan.block([(qkv_w, 2 * D + 512 * i, 512)], token=True) for i in range(2)]
        ao = [plan.block([(a["att_w_o_2"][0], 512 * i, 512)]) for i in range(2)]
        gate_up, down = [], []

        def plan_feed_forward(layer):
            w = a["ffn_w_gate_up_2"][layer]
            gate_up.append([])
            for i in range(FC // 2):
                gate_up[layer].append(plan.block([(w, 256 * i, 256), (w, FF + 256 * i, 256)],
                                                 low=gp if layer == 0 else both))
                if layer == 0:
                    ada_tiles(1)
            down.append([plan.block([(a["ffn_w_down_2"][layer], 512 * i, 512)], rows=FF) for i in range(2)])

        plan_feed_forward(0)
        ada_tiles(1)
        rq = [plan.block([(ret_w, 512 * i, 512)]) for i in range(2)]
        rk = [plan.block([(ret_w, D + 512 * i, 512)]) for i in range(2)]
        rv = [plan.block([(ret_w, 2 * D + 512 * i, 512)], token=True) for i in range(4)]
        rg = [plan.block([(ret_w, 4 * D + 512 * i, 512)]) for i in range(4)]
        ro = [plan.block([(a["ret_w_o_2"][0], 512 * i, 512)], rows=2 * D) for i in range(2)]
        plan_feed_forward(1)

        loaded = [sem(f"loaded{i}") for i in range(RING)]
        evac = [sem(f"evacuated{i}") for i in range(BANKS)]
        mloaded = [sem(f"expert_loaded{i}") for i in range(ERING)]

        def at(t):
            return ring[t.slot]

        def ahead(g):
            return min(plan.unit_of[g] + HIGHS - 1, (UNITS1 if plan.unit_of[g] < UNITS1 else len(plan.units)) - 1)

        def low_part(u):
            return ring_low[u.tile.slot][:, :, u.j * HALF:(u.j + 1) * HALF]

        def wait_evac(eng, g):
            eng.wait_ge(evac[g % BANKS], g // BANKS + 1)

        def wait_evac_all(eng, blocks):
            gs = [g for b in blocks for g in b.groups]
            for g in gs[-BANKS:]:
                wait_evac(eng, g)

        def half(b):
            return b.rearrange("p (c t) -> p c t", c=2)

        def row(t):
            return t.rearrange("p (o t) -> p o t", o=1).to_broadcast([P, DC, T])

        def cut(o, n):
            return arena[:, o:o + n]

        h_tok = big(1).rearrange("p c t -> p (c t)").rearrange("p (i f) -> p i f", i=TT)
        acc = big(2)
        e0 = 3 * DC * T
        xg_s, xgT = cut(e0, 512), cut(e0 + 512, 512).rearrange("p (h c j) -> p h c j", h=2, c=4)
        gu_s = [cut(e0 + 1024 + 512 * i, 512) for i in range(2)]
        gu_t = [cut(e0 + 2048 + 512 * i, 512) for i in range(2)]
        sig = [cut(e0 + 3072 + 256 * i, 256) for i in range(2)]
        actT = cut(e0 + 3584, 512).rearrange("p (c j) -> p c j", c=DC)
        y_s, GT = cut(e0 + 4096, 512), cut(e0 + 4608, 256)
        Ssel = [cut(e0 + 4864 + 64 * i, 64) for i in range(2)]
        Gsel = [cut(e0 + 4992 + 128 * i, 128) for i in range(2)]
        r0 = e0 + 5248
        rw = cut(r0, 256).rearrange("p (k e) -> p k e", k=DC)
        lgT, gateT = cut(r0 + 256, 256), cut(r0 + 512, 256)
        bdown = cv_pad[:, :, :].rearrange("p c t -> p (c t)")[:, RH * T:RH * T + D]
        r1 = r0 + 1792

        def pair32(k):
            return cut(r1 + 64 * k, 64).rearrange("p (i e) -> p i e", i=2)

        lg, mask, ex, gates, posr = [pair32(k) for k in range(5)]
        top8 = cut(r1 + 320, 16).rearrange("p (i e) -> p i e", i=2)
        idxf = cut(r1 + 336, 16).rearrange("p (i e) -> p i e", i=2)
        negm, den, rden, cmax, over = (cut(r1 + 352 + 2 * k, 2) for k in range(5))
        idx = sb("idx", [P, 2, 8], U32)
        nrounds = sb("nrounds", [P, 2], I32)

        c2 = a_pad[:, :, :].rearrange("p c t -> p (c t)")
        att_a = [c2[:, NC2 + 384 * i:NC2 + 384 * (i + 1)] for i in range(2)]
        dec = cv_pad[:, :, :].rearrange("p c t -> p (c t)")[:, 0:RH * T].rearrange("p (h t) -> p h t", h=RH)

        def k2(name, n=P):
            return c2[:, C2[name]:C2[name] + n]

        prob = [cut(scratch + 512 * h, 512) for h in range(XHEADS)]
        pT = [cut(DC * T + 512 * h, 512) for h in range(XHEADS)]
        xmax, xneg, xsum, xrec = (small[:, 8 * k:8 * k + 8] for k in range(4))
        bmax, bneg, bsum, brec = (small[:, 32 + 4 * k:36 + 4 * k] for k in range(4))
        NSB = 8
        attn2, q2, kk2 = big(1), big(3), big(4)
        v2 = big(5).rearrange("p c t -> p (c t)").rearrange("p (i f) -> p i f", i=TT)
        v2r = cut(5 * DC * T, 2 * DC * T).rearrange("p (i f) -> p i f", i=TT)
        hidden = (split_big(3, FC), split_big(3, FC, FC * T), None)
        ret_split = (split_big(3, 16), split_big(3, 16, FC * T))
        t0 = 7 * DC * T
        a_e, a_r, a_L, a_t, a_A = ([cut(t0 + 768 * k + 384 * i, 384) for i in range(2)] for k in range(5))
        rope_t = cut(t0, 512)
        ff_s = [cut(DC * T + 512 * i, 512) for i in range(2)]
        ff_h = [cut(DC * T + 1024 + 512 * i, 512) for i in range(2)]
        ret_o = cut(DC * T, 2 * DC * T).rearrange("p (c t) -> p c t", c=16)
        ret_g = cut(7 * DC * T, 2 * DC * T).rearrange("p (c t) -> p c t", c=16)
        ret_sq = cut(3 * DC * T, 2 * DC * T).rearrange("p (c t) -> p c t", c=16)
        rot_t = [cut(DC * T + 1024 * i, 1024).rearrange("p (h t) -> p h t", h=RH) for i in range(2)]
        gn_std = cv_pad[:, :, :].rearrange("p c t -> p (c t)")[:, RH * T:2 * RH * T].rearrange("p (h t) -> p h t", h=RH)

        splits = {}

        def split(name, src, high, low):
            splits[name] = (len(splits) + 1, src, high, low)
            return high, low, 2 * len(splits)

        sx = split("x", xT, x_high[:, :, :], x_low[:, :, :])
        s_gb = split("gate_b", gate_b, split_big(5), split_big(4))
        s_conv = split("conv", conv, split_big(3), split_big(2))
        s_m = split("mix", m_sum, split_big(5), split_big(7))
        s_mem = split("mem", memT, split_big(8), split_big(1))
        s_x1 = split("x1", xT, x_high[:, :, :], x_low[:, :, :])
        s_attn = split("attn", attn, x_high[:, :, :], x_low[:, :, :])
        s_h = [split("h0", big(2), x_high[:, :, :], x_low[:, :, :])]
        s_attn2 = split("attn2", attn2, x_high[:, :, :], x_low[:, :, :])
        s_h += [split("h1", big(2), x_high[:, :, :], x_low[:, :, :]), split("h2", big(2), x_high[:, :, :], x_low[:, :, :])]
        s_ret = split("ret", ret_o, *ret_split)
        s_h.append(split("h3", big(2), x_high[:, :, :], x_low[:, :, :]))

        def halves(x):
            n = x.shape[1] // 2
            return slice(0, n), slice(n, 2 * n)

        def units_of(*blocks):
            return [u.n for b in blocks for u in b.units]

        class Norm:
            count, centred = 0, 0

            def __init__(self, src, sq, dst, g, b, mean, eps_col, centre=True):
                self.src, self.sq, self.dst, self.g, self.b = src, sq, dst, g, b
                self.mean, self.eps = mean, eps[:, eps_col:eps_col + 1]
                self.n = Norm.count = Norm.count + 1
                if centre:
                    Norm.centred += 1
                self.c = Norm.centred if centre else None

        def cols(name):
            return lambda c: pc(name, c)

        n_mem = Norm(memT, sq, memT, cols("mem_ln_g"), cols("mem_ln_b"), mean_w, 0)
        n_conv = Norm(conv, sq, conv, cols("ln_a_g"), cols("ln_a_b"), mean_w, 0)
        n_1 = Norm(resid, big(5), xT, cols("ln1_g"), cols("ln1_b"), mean_w, 0)
        n_2 = Norm(resid, big(2), xT, cols("ln2_g"), cols("ln2_b"), mean_w, 0)
        n_3 = Norm(acc, big(1), xT, cols("ln3_g"), cols("ln3_b"), mean_w, 0)

        def mcol(layer, j):
            return lambda c: mod[:, 48 * layer + DC * j + c:48 * layer + DC * j + c + 1]

        def scol(k):
            return lambda c: gscale[:, DC * k + c:DC * k + c + 1]

        rms = [Norm(xT, big(1), big(2), scol(k), mcol(k // 2, 3 * (k % 2)), mean_w, 1, False) for k in range(4)]
        n_end = Norm(xT, big(1), big(2), cols("final_norm_2"), None, mean_w, 1, False)

        block = ctx.enter_context(nc.Block())

        @block.sync
        def _(sp):
            sp.dma_start(xT[:, 0:4, :], a["xT"][0:512, :].rearrange("(c p) t -> p c t", p=P)).then_inc(sem("x_in"), 16)
            sp.dma_start(xT[:, 4:8, :], a["xT"][512:D, :].rearrange("(c p) t -> p c t", p=P)).then_inc(sem("x_in"), 16)

            def load_tile(t):
                if t.n >= RING and not N1 <= t.n < N1 + RING:
                    for name, value in plan.tiles[t.n - RING].freed:
                        sp.wait_ge(sem(name), value)
                for w, at_col, kc in t.parts:
                    if w is None:
                        sp.dma_start(ring[t.slot][:, :, 0:256],
                                     a["pool_w"][0].rearrange("g (k p) n -> p (g k) n", p=P)).then_inc(loaded[t.slot], 16)
                    else:
                        sp.dma_start(ring[t.slot][:, 0:kc, at_col:at_col + w.shape[1]],
                                     w.rearrange("(k p) n -> p k n", p=P)).then_inc(loaded[t.slot], 16)

            load_tile(plan.tiles[0])
            sp.dma_start(par[:, :], params).then_inc(sem("par_in"), 16)
            for t in plan.tiles[1:4]:
                load_tile(t)
            sp.dma_start(memT, a["memT"].rearrange("(c p) t -> p c t", p=P)).then_inc(sem("mem_in"), 16)
            sp.dma_start(c1[:, :], consts1).then_inc(sem("c1_in"), 16)
            for t in plan.tiles[4:N1]:
                load_tile(t)

            def expert_tile(e, k):
                if k < 4:
                    src = a["w_gu"][0][e, :, D * (k % 2) + 512 * (k // 2):D * (k % 2) + 512 * (k // 2) + 512]
                else:
                    src = a["w_down"][0][e, :, 512 * (k - 4):512 * (k - 4) + 512]
                sp.dma_start(ring[k][:, :, :], src.rearrange("(k p) n -> p k n", p=P)).then_inc(mloaded[k], 16)

            final = {n % RING: n for n in range(N1)}
            for k in sorted(final, key=final.get) + list(range(RING, ERING)):
                if final.get(k) == xo[0].units[0].tile.n:
                    sp.wait_ge(sem("x_split"), s_attn[2])
                    sp.dma_start(rw, a["router_w"][0].rearrange("(k p) e -> p k e", p=P)).then_inc(sem("router_in"), 16)
                    sp.dma_start(bdown[0:NEXP, :], a["b_down"][0]).then_inc(sem("router_in"), 16)
                if k < RING:
                    for name, value in plan.tiles[final[k]].freed:
                        sp.wait_ge(sem(name), value)
                else:
                    sp.wait_ge(sem("mm_done"), PRODUCTS1)
                expert_tile(0, k)
            sp.wait_ge(sem("ln_out"), 2 * n_2.n)
            sp.dma_start(c2[:, 0:NC2], consts2).then_inc(sem("c2_in"), 16)
            sp.dma_start(dec, decay.rearrange("p (h t) -> p h t", h=RH)).then_inc(sem("c2_in"), 16)
            sp.wait_ge(sem("rounds_ready"), 1)
            n = sp.value_load(nrounds[0:1, 0:1], min_val=1, max_val=T // CAP)
            with sp.Fori(1, n * NEXP) as it:
                for k in range(ERING):
                    if k % 2 == 0:
                        sp.wait_ge(sem(("m_gu0", "m_gu1", "m_down")[k // 2]), it)
                    expert_tile(it % NEXP, k)
            for t in plan.tiles[N1:]:
                if t.n < N1 + RING:
                    sp.wait_ge(sem(("m_gu0", "m_gu1", "m_down")[t.slot // 2]), n * NEXP)
                load_tile(t)
            sp.wait_ge(sem("ln_out"), 2 * n_end.n)
            sp.dma_start(out.rearrange("(c p) t -> p c t", p=P), n_end.dst).then_inc(sem("out_stored"), 16)
            sp.wait_ge(sem("out_stored"), 16)

        @block.tensor
        def _(pe):
            def open_group(g):
                if g >= BANKS:
                    pe.wait_ge(evac[g % BANKS], g // BANKS)
                return bank[g % BANKS]

            def arrived(t):
                pe.wait_ge(loaded[t.slot], t.loaded)

            def split_ready(name):
                pe.wait_ge(sem("x_split"), 2 * splits[name][0] - 1)

            def feature(b, x):
                for u in b.units:
                    g = b.groups[u.j]
                    acc_bank = open_group(g) if u.k0 == 0 else bank[g % BANKS]
                    pe.wait_ge(sem(u.low), u.low_n)
                    high, low = w_high[u.n % HIGHS], low_part(u)
                    for ch in range(2):
                        for k in range(u.kc):
                            kk = u.k0 + k
                            if ch == 0 and u.j == 0 and kk == b.kc // 2 and x[2]:
                                pe.wait_ge(sem("x_split"), x[2])
                            for n, (w, xs) in enumerate(((high, x[0]), (high, x[1]), (low, x[0]))):
                                mm = pe.matmul(acc_bank[:, ch * T:(ch + 1) * T], w[:, k, ch * P:(ch + 1) * P],
                                               xs[:, kk, :], start=kk + ch + n == 0, stop=kk == b.kc - 1 and n == 2,
                                               skip_group_check=True)
                    mm.then_inc(sem("mm_done"), 1)

            def token(b, x):
                for u in b.units:
                    high, low = w_high[u.n % HIGHS], low_part(u)
                    for i, g in enumerate(b.groups):
                        acc_bank = open_group(g) if u.j == 0 else bank[g % BANKS]
                        if i == 0:
                            pe.wait_ge(sem(u.low), u.low_n)
                        for k in range(DC):
                            if i + u.j == 0 and k == DC // 2:
                                pe.wait_ge(sem("x_split"), x[2])
                            for n, (xs, w) in enumerate(((x[0], high), (x[0], low), (x[1], high))):
                                mm = pe.matmul(acc_bank[:, u.j * HALF:(u.j + 1) * HALF], xs[:, k, i * P:(i + 1) * P],
                                               w[:, k, :], start=k + u.j + n == 0, stop=k == DC - 1 and n == 2,
                                               skip_group_check=True)
                    mm.then_inc(sem("mm_done"), 1)

            def norm_mean(n):
                for c in range(DC):
                    mm = pe.matmul(bank[4][:, 0:T], n.mean[:, :], n.src[:, c, :], start=c == 0, stop=c == DC - 1)
                mm.then_inc(sem("ln_mean"), 1)

            def norm_var(n):
                for c in range(DC):
                    if c % (DC // 2) == 0:
                        pe.wait_ge(sem("ln_sq"), 2 * n.n - 1 + c // (DC // 2))
                    mm = pe.matmul(bank[5][:, 0:T], n.mean[:, :], n.sq[:, c, :], start=c == 0, stop=c == DC - 1)
                mm.then_inc(sem("ln_var"), 1)

            def ada_reduce(i):
                pe.wait_ge(sem("ada_taken"), i + 1)
                for q in range(4):
                    mm = pe.matmul(bank[7][:, 4 * i + q:4 * i + q + 1], ada_acc[i % 2][:, q * P:(q + 1) * P],
                                   ones[:, 0:1], start=True, stop=True)
                mm.then_inc(sem("ada_reduced"), 1)

            pe.wait_ge(sem("consts_set"), 3)
            split_ready("x")
            for b in glu:
                feature(b, sx)
            pe.wait_ge(sem("mem_in"), 16)
            norm_mean(n_mem)
            for b in cv:
                feature(b, sx)
            norm_var(n_mem)
            for b in pi + gb:
                feature(b, sx)
            for i in range(2):
                feature(branch_gate["c", i], sx)
                if i == 0:
                    pe.wait_ge(sem("pooled_ready"), len(WINDOWS))
                    arrived(pool_tile)
                for j, g in enumerate(branch_out["c", i].groups):
                    acc_bank = open_group(g)
                    grp = 2 * i + j
                    for ch in range(2):
                        for kc in range(2):
                            mm = pe.matmul(acc_bank[:, ch * T:(ch + 1) * T],
                                           at(pool_tile)[:, 2 * grp + kc, ch * P:(ch + 1) * P],
                                           pooled[:, 2 * grp + kc, :], start=kc == 0, stop=kc == 1)
                    mm.then_inc(sem("mm_done"), 1)
            pe.wait_ge(sem("conv_step"), TAPS_A * DC)
            norm_mean(n_conv)
            feature(branch_gate["b", 0], sx)
            split_ready("gate_b")
            feature(branch_out["b", 0], s_gb)
            ada_reduce(0)
            norm_var(n_conv)
            feature(branch_gate["b", 1], sx)
            ada_reduce(1)
            feature(branch_out["b", 1], s_gb)
            ada_reduce(2)
            feature(branch_gate["a", 0], sx)
            ada_reduce(3)
            split_ready("conv")
            feature(branch_out["a", 0], s_conv)
            ada_reduce(4)
            feature(branch_gate["a", 1], sx)
            ada_reduce(5)
            feature(branch_out["a", 1], s_conv)
            ada_reduce(6)
            split_ready("mix")
            feature(mix[0], s_m)
            ada_reduce(7)
            feature(mix[1], s_m)
            ada_reduce(8)
            split_ready("mem")
            feature(xk[0], s_mem)
            wait_evac_all(pe, mix)
            norm_mean(n_1)
            ada_reduce(9)
            feature(xk[1], s_mem)
            norm_var(n_1)
            ada_reduce(10)
            ada_reduce(11)
            for b in xv:
                token(b, s_mem)
            split_ready("x1")
            for b in xq:
                feature(b, s_x1)
            wait_evac_all(pe, xk + xv + xq)
            pe.wait_ge(sem("mod_ready"), 1)
            for h in range(XHEADS):
                for i in range(TT):
                    for k in range(2):
                        mm = pe.matmul(bank[4 + h][:, i * T:(i + 1) * T], qT[:, 2 * h + k, i * P:(i + 1) * P],
                                       kT[:, 2 * h + k, :], start=k == 0, stop=k == 1)
                mm.then_inc(sem("x_scores"), 1)
            for h in range(XHEADS + 1):
                if h < XHEADS:
                    pe.wait_ge(sem("x_prob"), h + 1)
                    for j in range(TT):
                        for i in range(TT):
                            mm = pe.transpose(bank[4 + h][:, j * T + i * P:j * T + (i + 1) * P],
                                              half(prob[h])[:, i, j * P:(j + 1) * P], ident)
                    mm.then_inc(sem("x_turned"), 1)
                if h > 0:
                    pe.wait_ge(sem("x_pT"), h)
                    for c in range(2):
                        for j in range(TT):
                            f = XD * (h - 1) + P * c
                            mm = pe.matmul(bank[3 + h][:, c * T:(c + 1) * T], v_tok[:, j, f:f + P],
                                           half(pT[h - 1])[:, j, :], start=j == 0, stop=j == TT - 1)
                    mm.then_inc(sem("x_out"), 1)
            split_ready("attn")
            for b in xo:
                feature(b, s_attn)
            wait_evac_all(pe, xo)
            norm_mean(n_2)
            norm_var(n_2)
            pe.wait_ge(sem("ln_out"), 2 * n_2.n)

            pe.wait_ge(sem("router_in"), 32)
            for k in range(DC):
                mm = pe.matmul(bank[4][0:NEXP, 0:T], rw[:, k, :], xT[:, k, :], start=k == 0, stop=k == DC - 1)
            mm.then_inc(sem("r_logitsT"), 1)
            for q in range(4):
                for c in range(4):
                    i, f = q // 2, 4 * (q % 2) + c
                    mm = pe.transpose(bank[q][:, c * P:(c + 1) * P], xT[:, f, i * P:(i + 1) * P], ident)
                mm.then_inc(sem("r_tok"), 1)
            pe.wait_ge(sem("r_lgT"), 1)
            for i in range(TT):
                mm = pe.matmul(bank[5][:, i * NEXP:(i + 1) * NEXP], lgT[0:NEXP, i * P:(i + 1) * P],
                               ident[0:NEXP, 0:NEXP], start=True, stop=True)
            mm.then_inc(sem("r_logits"), 1)
            pe.wait_ge(sem("r_mask"), 1)
            pe.matmul(bank[6][:, 0:NEXP], k1("before"), mask[:, 0, :], start=True, stop=True)
            pe.matmul(bank[6][:, NEXP:2 * NEXP], ones[:, :], mask[:, 0, :], start=True, stop=False)
            pe.matmul(bank[6][:, NEXP:2 * NEXP], k1("before"), mask[:, 1, :], start=False, stop=True)
            pe.matmul(bank[6][:, 2 * NEXP:3 * NEXP], ones[:, :], mask[:, 0, :], start=True, stop=False)
            pe.matmul(bank[6][:, 2 * NEXP:3 * NEXP], ones[:, :], mask[:, 1, :], start=False,
                      stop=True).then_inc(sem("r_pos"), 1)
            pe.wait_ge(sem("r_gates"), 1)
            for i in range(TT):
                mm = pe.matmul(bank[7][0:NEXP, i * P:(i + 1) * P], gates[:, i, :], ident, start=True, stop=True)
            mm.then_inc(sem("r_gateT"), 1)
            pe.wait_ge(sem("r_gateT_in"), 1)
            pe.wait_ge(sem("r_tok_in"), 4)
            for q in range(4):
                for ch in range(2):
                    c = 2 * q + ch
                    mm = pe.matmul(bank[q][:, ch * T:(ch + 1) * T], bdown[0:NEXP, c * P:(c + 1) * P],
                                   gateT[0:NEXP, :], start=True, stop=True)
                mm.then_inc(sem("r_bias"), 1)
            pe.wait_ge(sem("m_acc"), 4)
            pe.wait_ge(sem("rounds_ready"), 1)
            n = pe.value_load(nrounds[0:1, 0:1], min_val=1, max_val=T // CAP)

            def gather(it):
                pe.wait_ge(sem("m_sel"), it + 1)
                for i in range(TT):
                    for o in range(2):
                        mm = pe.matmul(bank[4][64 * o:64 * o + 64, :], Ssel[i],
                                       h_tok[:, i, 512 * o:512 * o + 512], start=i == 0, stop=i == TT - 1)
                mm.then_inc(sem("m_gather"), 1)

            def turn_inputs(it):
                pe.wait_ge(sem("m_xg"), it + 1)
                for c in range(4):
                    mm = pe.transpose(bank[6][:, c * P:(c + 1) * P], xg_s[:, c * P:(c + 1) * P], ident)
                mm.then_inc(sem("m_xturn"), 1)

            def gate_up_half(it, b):
                for k in (2 * b, 2 * b + 1):
                    pe.wait_ge(mloaded[k], (it + 1) * 16)
                for k in range(DC):
                    for o in range(2):
                        mm = pe.matmul(bank[b][64 * o:64 * o + 64, :], xgT[:, k // 4, k % 4, :],
                                       ring[2 * b + o][:, k, :], start=k == 0, stop=k == DC - 1)
                mm.then_inc(sem(f"m_gu{b}"), 1)

            def turn_half(it, b):
                pe.wait_ge(sem("m_gus"), it * 2 + (b + 1))
                for c in range(4):
                    mm = pe.transpose(bank[2 + b][:, c * P:(c + 1) * P], gu_s[b][:, c * P:(c + 1) * P], ident)
                mm.then_inc(sem("m_guturn"), 1)

            def turn_gates(it):
                pe.wait_ge(sem("m_gsel"), it + 1)
                for i in range(TT):
                    mm = pe.transpose(bank[5][:, i * P:(i + 1) * P], Gsel[i], ident)
                mm.then_inc(sem("m_gturn"), 1)

            def down_proj(it):
                for k in (4, 5):
                    pe.wait_ge(mloaded[k], (it + 1) * 16)
                for k in range(DC):
                    if k % 4 == 0:
                        pe.wait_ge(sem("m_act"), it * 2 + (k // 4 + 1))
                    for o in range(2):
                        mm = pe.matmul(bank[7][64 * o:64 * o + 64, :], actT[:, k, :], ring[4 + o][:, k, :],
                                       start=k == 0, stop=k == DC - 1)
                mm.then_inc(sem("m_down"), 1)

            def scatter(it):
                pe.wait_ge(sem("m_ys"), it + 1)
                pe.wait_ge(sem("m_gt"), it + 1)
                for q in range(4):
                    for ch in range(2):
                        c = 2 * q + ch
                        o = 64 * (c // 4)
                        mm = pe.matmul(bank[4 + q][:, ch * T:(ch + 1) * T], y_s[o:o + 64, (c % 4) * P:(c % 4 + 1) * P],
                                       GT[o:o + 64, :], start=True, stop=True)
                    mm.then_inc(sem("m_scatter"), 1)

            def enter_expert(it):
                pe.wait_ge(sem("m_xgT"), it + 1)
                gate_up_half(it, 0)

            gather(0)
            turn_inputs(0)
            enter_expert(0)
            last = pe.value_load(nrounds[0:1, 1:2], min_val=NEXP - 1, max_val=T // CAP * NEXP - 1)
            with pe.Fori(0, last) as it:
                gate_up_half(it, 1)
                turn_half(it, 0)
                pe.wait_ge(sem("m_acc"), it * 4 + 4)
                gather(it + 1)
                turn_half(it, 1)
                turn_inputs(it + 1)
                turn_gates(it)
                down_proj(it)
                enter_expert(it + 1)
                scatter(it)
            gate_up_half(last, 1)
            turn_half(last, 0)
            turn_half(last, 1)
            pe.wait_ge(sem("m_acc"), last * 4 + 4)
            turn_gates(last)
            down_proj(last)
            scatter(last)
            pe.wait_ge(sem("m_acc"), n * (4 * NEXP) + 4)
            norm_mean(n_3)
            norm_var(n_3)

            def rms_norm(n):
                pe.wait_ge(sem("ln_out"), 2 * (n.n - 1))
                norm_var(n)
                pe.wait_ge(sem("ln_out"), 2 * n.n)

            def causal_out(dst, v_cols, probs, n_rows=P):
                pe.matmul(dst[:, 0:T], v_cols(0), probs[:, 0:T], start=True, stop=False)
                return pe.matmul(dst[:, P:T], v_cols(1), probs[:, T:T + P], start=False, stop=True)

            rms_norm(rms[0])
            split_ready("h0")
            for b in aq + ak:
                feature(b, s_h[0])
            for b in av:
                token(b, s_h[0])
            pe.wait_ge(sem("c2_in"), 32)
            wait_evac_all(pe, ak)
            for n_, X in enumerate((q2, kk2)):
                for p_ in range(2):
                    for ch in range(2):
                        mm = pe.matmul(bank[4 + 2 * n_ + p_][:, ch * T:(ch + 1) * T], k2("swap"),
                                       X[:, 4 + 2 * p_ + ch, :], start=True, stop=True)
                    mm.then_inc(sem("rope_mm"), 1)
            wait_evac_all(pe, av)
            pe.wait_ge(sem("roped"), 4)

            def head_rows(h):
                return slice(HD * (h % 2), HD * (h % 2) + HD), h // 2

            for i in range(NSB + 2):
                if i < NSB:
                    r, c = head_rows(i)
                    if i >= 2:
                        pe.wait_ge(sem("a_L"), i - 1)
                    b = bank[4 + i % 2]
                    pe.matmul(b[:, 0:T], kk2[r, c, 0:P], q2[r, c, :], start=True, stop=True)
                    pe.matmul(b[:, T:T + P], kk2[r, c, P:T], q2[r, c, P:T], start=True,
                              stop=True).then_inc(sem("a_z"), 1)
                if 1 <= i <= NSB:
                    h = i - 1
                    pe.wait_ge(sem("a_L"), h + 1)
                    if h >= 1:
                        pe.wait_ge(sem("a_t"), h)
                    L = a_L[h % 2]
                    pe.matmul(bank[6][:, 0:T], k1("later"), L[:, 0:T], start=True, stop=False)
                    pe.matmul(bank[6][:, P:T], ones[:, :], L[:, T:T + P], start=False, stop=True)
                    pe.matmul(bank[6][:, T:T + P], k1("later"), L[:, T:T + P], start=True,
                              stop=True).then_inc(sem("a_after"), 1)
                if i >= 2:
                    h = i - 2
                    r, c = head_rows(h)
                    pe.wait_ge(sem("a_A"), h + 1)
                    if h % 2 == 0 and h >= 2:
                        pe.wait_ge(sem("a_oT"), h // 2)
                    causal_out(bank[7][r, :], lambda j: v2[:, j, HD * h:HD * h + HD], a_A[h % 2]).then_inc(sem("a_o"), 1)
            pe.wait_ge(sem("a_oT"), NSB // 2)
            for i in range(NSB + 2):
                if i < NSB:
                    r, c = head_rows(NSB + i)
                    if i >= 2:
                        pe.wait_ge(sem("b_max"), i - 1)
                    b = bank[4 + i % 2]
                    pe.matmul(b[:, 0:P], q2[r, c, 0:P], kk2[r, c, 0:P], start=True, stop=True)
                    pe.matmul(b[:, P:P + T], q2[r, c, P:T], kk2[r, c, :], start=True,
                              stop=True).then_inc(sem("b_s"), 1)
                if 1 <= i <= NSB:
                    h = i - 1
                    pe.wait_ge(sem("b_prob"), h + 1)
                    if h >= 1:
                        pe.wait_ge(sem("b_pT"), h)
                    pr = a_t[h % 2]
                    pe.transpose(bank[6][:, 0:P], pr[:, 0:P], ident)
                    pe.transpose(bank[6][:, P:T], pr[:, P:T], ident)
                    pe.transpose(bank[6][:, T:T + P], pr[:, T:T + P], ident).then_inc(sem("b_turned"), 1)
                if i >= 2:
                    h = i - 2
                    r, c = head_rows(h)
                    pe.wait_ge(sem("b_pT"), h + 1)
                    if h % 2 == 0 and h >= 2:
                        pe.wait_ge(sem("b_oT"), h // 2)
                    causal_out(bank[7][r, :], lambda j: v2[:, j, HD * (NSB + h):HD * (NSB + h) + HD],
                               a_A[h % 2]).then_inc(sem("b_o"), 1)
            pe.wait_ge(sem("b_oT"), NSB // 2)
            split_ready("attn2")
            for b in ao:
                feature(b, s_attn2)
            wait_evac_all(pe, ao)

            def feed_forward(layer):
                norm_var(rms[2 * layer + 1])
                split_ready(("h1", "h3")[layer])
                for i, b in enumerate(gate_up[layer]):
                    feature(b, s_h[2 * layer + 1])
                    if layer == 0 and i:
                        ada_reduce(12 + i - 1)
                pe.wait_ge(sem("ff_hidden"), (layer + 1) * FC // 2)
                for b in down[layer]:
                    feature(b, hidden)
                if layer == 0:
                    ada_reduce(22)
                    ada_reduce(23)
                    pe.wait_ge(sem("mod_ready"), 2)
                wait_evac_all(pe, down[layer])

            feed_forward(0)
            norm_var(rms[2])
            split_ready("h2")
            for b in rq + rk:
                feature(b, s_h[2])
            for b in rv:
                token(b, s_h[2])
            for b in rg:
                feature(b, s_h[2])
            pe.wait_ge(sem("ret_rot"), 2)
            wait_evac_all(pe, rv + rg)
            for i in range(RH + 1):
                if i < RH:
                    b = bank[4 + i % 2]
                    if i >= 2:
                        pe.wait_ge(sem("ret_inner"), i - 1)
                    for k in range(2):
                        pe.matmul(b[:, 0:T], kk2[:, 2 * i + k, 0:P], q2[:, 2 * i + k, :], start=k == 0, stop=k == 1)
                    for k in range(2):
                        mm = pe.matmul(b[:, T:T + P], kk2[:, 2 * i + k, P:T], q2[:, 2 * i + k, P:T], start=k == 0,
                                       stop=k == 1)
                    mm.then_inc(sem("ret_s"), 1)
                if i >= 1:
                    h = i - 1
                    pe.wait_ge(sem("ret_inner"), h + 1)
                    for cp in range(2):
                        n_ = 2 * h + cp
                        if n_ >= 2:
                            pe.wait_ge(sem("ret_o"), n_ - 1)
                        for ch in range(2):
                            f = RV * h + P * (2 * cp + ch)
                            mm = causal_out(bank[6 + n_ % 2][:, ch * T:(ch + 1) * T],
                                            lambda j: v2r[:, j, f:f + P], att_a[h % 2])
                        mm.then_inc(sem("ret_omm"), 1)
            pe.wait_ge(sem("ret_o"), 2 * RH)
            for src, done, need in ((ret_o, "gn_mean", None), (ret_sq, "gn_var", "gn_sq")):
                for h in range(RH):
                    b = bank[(4 if done == "gn_mean" else 6) + h // 2]
                    if need:
                        pe.wait_ge(sem(need), h + 1)
                    for c in range(4):
                        mm = pe.matmul(b[:, (h % 2) * T:(h % 2 + 1) * T], mean_v[:, :], src[:, 4 * h + c, :],
                                       start=c == 0, stop=c == 3)
                    if h % 2:
                        mm.then_inc(sem(done), 1)
            split_ready("ret")
            for b in ro:
                feature(b, s_ret)
            wait_evac_all(pe, ro)
            feed_forward(1)
            norm_var(n_end)

        @block.scalar
        def _(act):
            steps = [0]

            def link(ins):
                steps[0] += 1
                ins.then_inc(sem("act_step"), 1)
                act.wait_ge(sem("act_step"), steps[0])

            highs = [0]

            def high_until(n):
                while highs[0] <= n:
                    u = plan.units[highs[0]]
                    act.wait_ge(loaded[u.tile.slot], u.tile.loaded)
                    if u.n >= HIGHS:
                        act.wait_ge(sem("mm_done"), plan.units[u.n - HIGHS].done)
                    nc.scalar.activation(w_high[u.n % HIGHS][:, 0:u.kc, :], at(u.tile)[:, 0:u.kc, u.j * HALF:(u.j + 1) * HALF],
                                         ACT.Copy).then_inc(sem("w_high"), 1)
                    highs[0] += 1

            def split_high(name, norm=None):
                n, src, high, _ = splits[name]
                if n > 1:
                    act.wait_ge(sem("x_split"), 2 * (n - 1))
                for i, c in enumerate(halves(src)):
                    if norm:
                        act.wait_ge(sem("ln_out"), 2 * norm.n - 1 + i)
                    if name == "ret":
                        act.wait_ge(sem("gn_out"), i + 1)
                    nc.scalar.activation(high[:, c, :], src[:, c, :], ACT.Copy).then_inc(sem("x_high"), 1)

            def complete(g):
                if g in plan.unit_of:
                    high_until(ahead(g))
                act.wait_ge(sem("mm_done"), plan.done[g])

            def group(g, op):
                complete(g)
                for ch in range(2):
                    ins = op(ch, bank[g % BANKS][:, ch * T:(ch + 1) * T])
                ins.then_inc(evac[g % BANKS], 1)

            def copy_group(g, dst):
                complete(g)
                nc.scalar.activation(dst, bank[g % BANKS][:, :], ACT.Copy).then_inc(evac[g % BANKS], 1)

            def copy_features(blocks, dst):
                for i, b in enumerate(blocks):
                    for j, g in enumerate(b.groups):
                        copy_group(g, dst[:, 4 * i + 2 * j:4 * i + 2 * j + 2, :].rearrange("p c t -> p (c t)"))

            def copy_tokens(blocks, dst):
                for i, b in enumerate(blocks):
                    for j, g in enumerate(b.groups):
                        copy_group(g, dst[:, j, 512 * i:512 * i + 512])

            def norm_square(n, blocks=None):
                if n.c:
                    act.wait_ge(sem("ln_cen"), n.c)
                for i, c in enumerate(halves(n.src)):
                    if blocks:
                        wait_evac_all(act, blocks[i:i + 1])
                    nc.scalar.activation(n.sq[:, c, :], n.src[:, c, :], ACT.Square).then_inc(sem("ln_sq"), 1)

            def norm_std(n):
                act.wait_ge(sem("ln_var"), n.n)
                if n.n > 1:
                    act.wait_ge(sem("ln_out"), 2 * (n.n - 1))
                nc.scalar.activation(rstd[:, :], bank[5][:, 0:T], ACT.Sqrt, bias=n.eps).then_inc(sem("ln_std"), 1)

            act.wait_ge(sem("consts_set"), 3)
            act.wait_ge(sem("x_in"), 32)
            split_high("x")
            high_until(1)
            act.wait_ge(sem("par_in"), 16)
            nc.scalar.activation(silu_c[:, :], pc("c_2", 0, DC), ACT.Silu).then_inc(sem("silu_c"), 1)
            for i, b in enumerate(glu):
                if i >= 2:
                    wait_evac(act, glu[i - 2].groups[1])
                group(b.groups[0], lambda ch, ps: nc.scalar.activation(
                    sg[i % 2][:, ch * T:(ch + 1) * T], ps, ACT.Sigmoid, bias=pc("b_in", O_SIG // P + 2 * i + ch)))
            high_until(units_of(cv[0])[1])
            norm_square(n_mem)
            for i, b in enumerate(cv):
                if i < 2:
                    wait_evac(act, glu[i + 2].groups[1])
                else:
                    act.wait_ge(sem("cv_ready"), i - 1)
                group(b.groups[0], lambda ch, ps: nc.scalar.activation(
                    sg[i % 2][:, ch * T:(ch + 1) * T], ps, ACT.Identity, bias=pc("b_in", O_GC // P + 2 * i + ch)))
                group(b.groups[1], lambda ch, ps: nc.scalar.activation(
                    yb[i % 2][:, ch * T:(ch + 1) * T], ps, ACT.Identity, bias=pc("b_in", O_V // P + 2 * i + ch)))
            high_until(units_of(pi[0])[1])
            norm_std(n_mem)
            act.wait_ge(sem("cv_ready"), 4)
            for i, b in enumerate(pi):
                for j, g in enumerate(b.groups):
                    group(g, lambda ch, ps: nc.scalar.activation(
                        pool_in[:, 4 * i + 2 * j + ch, PADW:], ps, ACT.Identity,
                        bias=pc("b_in", O_POOL // P + 4 * i + 2 * j + ch)))
            for i, b in enumerate(gb):
                for j, g in enumerate(b.groups):
                    group(g, lambda ch, ps: nc.scalar.activation(
                        gate_b[:, 4 * i + 2 * j + ch, :], ps, ACT.Identity,
                        bias=pc("b_in", O_GB // P + 4 * i + 2 * j + ch)))
            high_until(units_of(branch_gate["c", 0])[1])
            act.wait_ge(sem("pooled_ready"), len(WINDOWS))

            def branch(name, k, i, off, out_op):
                for j, g in enumerate(branch_gate[name, i].groups):
                    n = 4 * k + 2 * i + j
                    if n >= 2:
                        act.wait_ge(sem("mixed"), n - 1)
                    group(g, lambda ch, ps: nc.scalar.activation(
                        sg[n % 2][:, ch * T:(ch + 1) * T], ps, ACT.Sigmoid,
                        bias=pc("b_in", (O_G + off) // P + 4 * i + 2 * j + ch)))
                for j, g in enumerate(branch_out[name, i].groups):
                    n = 4 * k + 2 * i + j
                    group(g, lambda ch, ps: out_op(yb[n % 2][:, ch * T:(ch + 1) * T], ps, 4 * i + 2 * j + ch))

            for i in range(2):
                branch("c", 0, i, 2 * D, lambda o, ps, c: nc.scalar.activation(
                    o, ps, ACT.Copy, scale=pc("pool_scale", c)))
            high_until(units_of(branch_gate["b", 0])[1])
            norm_square(n_conv)
            act.wait_ge(sem("gated"), 1)
            split_high("gate_b")
            branch("b", 1, 0, D, lambda o, ps, c: nc.scalar.activation(o, ps, ACT.Copy))
            high_until(units_of(branch_gate["b", 1])[1])
            norm_std(n_conv)
            branch("b", 1, 1, D, lambda o, ps, c: nc.scalar.activation(o, ps, ACT.Copy))
            high_until(units_of(branch_gate["a", 0])[1])
            act.wait_ge(sem("ln_out"), 2 * n_conv.n)
            for c in range(DC):
                ins = nc.scalar.activation(conv[:, c, :], conv[:, c, :], ACT.Silu, bias=n_conv.b(c), scale=n_conv.g(c))
            ins.then_inc(sem("silu_a"), 1)
            act.wait_ge(sem("silu_a"), 1)
            split_high("conv")
            for i in range(2):
                branch("a", 2, i, 0, lambda o, ps, c: nc.scalar.activation(
                    o, ps, ACT.Identity, bias=pc("b_a_out", c)))
            high_until(units_of(mix[0])[1])
            act.wait_ge(sem("mixed"), 12)
            split_high("mix")
            split_high("mem")
            high_until(units_of(xk[0])[1])
            copy_features(xk[:1], kT)
            high_until(units_of(xk[1])[1])
            norm_square(n_1)
            copy_features(xk[1:], kT[:, 4:8, :])
            high_until(units_of(xv[0])[1])
            norm_std(n_1)
            split_high("x1", n_1)
            copy_tokens(xv, v_tok)
            copy_features(xq, qT)
            high_until(units_of(xo[0])[1])
            for h in range(XHEADS):
                act.wait_ge(sem("x_max"), h + 1)
                for i in range(TT):
                    ins = nc.scalar.activation(half(prob[h])[:, i, :], bank[4 + h][:, i * T:(i + 1) * T], ACT.Exp,
                                               bias=xneg[:, 2 * h + i:2 * h + i + 1], scale=XD ** -0.5,
                                               accum_out=xsum[:, 2 * h + i:2 * h + i + 1])
                ins.then_inc(sem("x_exp"), 1)
            for h in range(XHEADS + 1):
                if h < XHEADS:
                    act.wait_ge(sem("x_turned"), h + 1)
                    nc.scalar.activation(pT[h], bank[4 + h][:, :], ACT.Copy).then_inc(sem("x_pT"), 1)
                if h > 0:
                    act.wait_ge(sem("x_out"), h)
                    nc.scalar.activation(attn[:, 2 * h - 2:2 * h, :].rearrange("p c t -> p (c t)"), bank[3 + h][:, :],
                                         ACT.Copy).then_inc(sem("x_oT"), 1)
            act.wait_ge(sem("x_oT"), XHEADS)
            split_high("attn")
            high_until(units_of(xo[1])[1])
            norm_square(n_2)
            norm_std(n_2)
            act.wait_ge(sem("r_logitsT"), 1)
            nc.scalar.activation(lgT[0:NEXP, :], bank[4][0:NEXP, 0:T], ACT.Copy).then_inc(sem("r_lgT"), 1)
            for q in range(4):
                act.wait_ge(sem("r_tok"), q + 1)
                nc.scalar.activation(h_tok[:, q // 2, 512 * (q % 2):512 * (q % 2) + 512], bank[q][:, :],
                                     ACT.Copy).then_inc(sem("r_tok_in"), 1)
            act.wait_ge(sem("r_top"), 1)
            for i in range(TT):
                ins = nc.scalar.activation(ex[:, i, :], lg[:, i, :], ACT.Exp, bias=negm[:, i:i + 1])
            ins.then_inc(sem("r_exp"), 1)
            act.wait_ge(sem("r_gateT"), 1)
            nc.scalar.activation(gateT[0:NEXP, :], bank[7][0:NEXP, 0:T], ACT.Copy).then_inc(sem("r_gateT_in"), 1)
            act.wait_ge(sem("rounds_ready"), 1)

            def rows_in(it):
                act.wait_ge(sem("m_gather"), it + 1)
                nc.scalar.activation(xg_s, bank[4][:, :], ACT.Copy).then_inc(sem("m_xg"), 1)

            def inputs_in(it):
                act.wait_ge(sem("m_xturn"), it + 1)
                nc.scalar.activation(xgT.rearrange("p h c j -> p c h j"),
                                     bank[6][:, :].rearrange("p (c h j) -> p c h j", c=4, h=2),
                                     ACT.Copy).then_inc(sem("m_xgT"), 1)

            def half_in(it, b):
                act.wait_ge(sem(f"m_gu{b}"), it + 1)
                nc.scalar.activation(gu_s[b], bank[b][:, :], ACT.Copy).then_inc(sem("m_gus"), 1)

            def sigmoid_half(it, b):
                act.wait_ge(sem("m_gate"), it * 2 + (b + 1))
                nc.scalar.activation(sig[b].rearrange("p (c j) -> p c j", c=4),
                                     gu_t[b].rearrange("p (c g j) -> p c g j", c=4, g=2)[:, :, 0, :],
                                     ACT.Sigmoid, scale=SWISH).then_inc(sem("m_sig"), 1)

            def outputs_in(it):
                act.wait_ge(sem("m_gturn"), it + 1)
                nc.scalar.activation(GT, bank[5][:, 0:T], ACT.Copy).then_inc(sem("m_gt"), 1)
                act.wait_ge(sem("m_down"), it + 1)
                nc.scalar.activation(y_s, bank[7][:, :], ACT.Copy).then_inc(sem("m_ys"), 1)

            rows_in(0)
            inputs_in(0)
            half_in(0, 0)
            last = act.value_load(nrounds[0:1, 1:2], min_val=NEXP - 1, max_val=T // CAP * NEXP - 1)
            with act.Fori(0, last) as it:
                half_in(it, 1)
                sigmoid_half(it, 0)
                rows_in(it + 1)
                inputs_in(it + 1)
                sigmoid_half(it, 1)
                outputs_in(it)
                half_in(it + 1, 0)
            half_in(last, 1)
            sigmoid_half(last, 0)
            sigmoid_half(last, 1)
            outputs_in(last)
            norm_square(n_3)
            norm_std(n_3)

            def rms_norm(n):
                act.wait_ge(sem("ln_out"), 2 * (n.n - 1))
                norm_square(n)
                norm_std(n)

            high_until(units_of(aq[0])[1])
            rms_norm(rms[0])
            split_high("h0", rms[0])
            copy_features(aq, q2)
            copy_features(ak, kk2)
            copy_tokens(av, v2)
            high_until(units_of(ao[0])[1])
            act.wait_ge(sem("roped"), 4)
            for i in range(NSB + 1):
                if i < NSB:
                    act.wait_ge(sem("a_z"), i + 1)
                    if i >= 2:
                        act.wait_ge(sem("a_L"), i - 1)
                    z = bank[4 + i % 2][:, 0:384]
                    link(nc.scalar.activation(a_e[i % 2], z, ACT.Abs))
                    link(nc.scalar.activation(a_e[i % 2], a_e[i % 2], ACT.Exp, scale=-HD ** -0.5))
                    link(nc.scalar.activation(a_e[i % 2], a_e[i % 2], ACT.Ln, bias=1.0))
                    nc.scalar.activation(a_r[i % 2], z, ACT.Relu, scale=HD ** -0.5).then_inc(sem("a_sp"), 1)
                if i >= 1:
                    h = i - 1
                    act.wait_ge(sem("a_t"), h + 1)
                    if h >= 2:
                        act.wait_ge(sem("a_o"), h - 1)
                    nc.scalar.activation(a_A[h % 2], a_t[h % 2], ACT.Exp).then_inc(sem("a_exp"), 1)
            act.wait_ge(sem("a_oT"), NSB // 2)
            for i in range(NSB + 1):
                if i < NSB:
                    act.wait_ge(sem("b_max"), i + 1)
                    k = i % 2
                    nc.scalar.activation(a_t[k][:, 0:P], a_L[k][:, 0:P], ACT.Exp, bias=bneg[:, 2 * k:2 * k + 1],
                                         accum_out=bsum[:, 2 * k:2 * k + 1])
                    nc.scalar.activation(a_t[k][:, P:P + T], a_L[k][:, P:P + T], ACT.Exp,
                                         bias=bneg[:, 2 * k + 1:2 * k + 2],
                                         accum_out=bsum[:, 2 * k + 1:2 * k + 2]).then_inc(sem("b_exp"), 1)
                if i >= 1:
                    h = i - 1
                    act.wait_ge(sem("b_turned"), h + 1)
                    if h >= 2:
                        act.wait_ge(sem("b_o"), h - 1)
                    nc.scalar.activation(a_A[h % 2], bank[6][:, 0:384], ACT.Copy).then_inc(sem("b_pT"), 1)

            def feed_forward(layer, before):
                norm_square(rms[2 * layer + 1], before)
                norm_std(rms[2 * layer + 1])
                split_high(("h1", "h3")[layer], rms[2 * layer + 1])
                for i, b in enumerate(gate_up[layer]):
                    m = layer * (FC // 2) + i
                    if i >= 2:
                        act.wait_ge(sem("ff_hidden"), m - 1)
                    g = b.groups[0]
                    complete(g)
                    nc.scalar.activation(ff_s[i % 2], bank[g % BANKS][:, :], ACT.Silu).then_inc(evac[g % BANKS], 1)

            act.wait_ge(sem("b_oT"), NSB // 2)
            split_high("attn2")
            high_until(units_of(gate_up[0][0])[1])
            feed_forward(0, ao)
            high_until(units_of(rq[0])[1])
            norm_square(rms[2], down[0])
            norm_std(rms[2])
            split_high("h2", rms[2])
            copy_features(rq, q2)
            copy_features(rk, kk2)
            copy_tokens(rv, v2r)
            for i, b in enumerate(rg):
                for j, g in enumerate(b.groups):
                    complete(g)
                    c = 4 * i + 2 * j
                    nc.scalar.activation(ret_g[:, c:c + 2, :].rearrange("p c t -> p (c t)"), bank[g % BANKS][:, :],
                                         ACT.Silu).then_inc(evac[g % BANKS], 1)
            high_until(units_of(ro[0])[1])
            for n_ in range(2 * RH):
                act.wait_ge(sem("ret_omm"), n_ + 1)
                if n_ == 0:
                    act.wait_ge(sem("ret_rot"), 2)
                nc.scalar.activation(ret_o[:, 2 * n_:2 * n_ + 2, :].rearrange("p c t -> p (c t)"),
                                     bank[6 + n_ % 2][:, :], ACT.Copy).then_inc(sem("ret_o"), 1)
            for h in range(RH):
                act.wait_ge(sem("gn_cen"), h + 1)
                nc.scalar.activation(ret_sq[:, 4 * h:4 * h + 4, :], ret_o[:, 4 * h:4 * h + 4, :],
                                     ACT.Square).then_inc(sem("gn_sq"), 1)
            for hp in range(2):
                act.wait_ge(sem("gn_var"), hp + 1)
                nc.scalar.activation(gn_std[:, 2 * hp:2 * hp + 2, :].rearrange("p c t -> p (c t)"), bank[6 + hp][:, :],
                                     ACT.Sqrt, bias=eps[:, 2:3]).then_inc(sem("gn_std"), 1)
            split_high("ret")
            high_until(units_of(gate_up[1][0])[1])
            feed_forward(1, ro)
            high_until(len(plan.units) - 1)
            norm_square(n_end, down[1])
            norm_std(n_end)

        @block.vector
        def _(dve):
            steps = [0]

            def link(ins):
                steps[0] += 1
                ins.then_inc(sem("dve_step"), 1)
                dve.wait_ge(sem("dve_step"), steps[0])

            V = nc.vector

            lows = [0]

            def low_until(n):
                while lows[0] <= n:
                    u = plan.units[lows[0]]
                    if u.low == "low_dve":
                        dve.wait_ge(sem("w_high"), u.n + 1)
                        V.tensor_tensor(low_part(u)[:, 0:u.kc, :], at(u.tile)[:, 0:u.kc, u.j * HALF:(u.j + 1) * HALF],
                                        w_high[u.n % HIGHS][:, 0:u.kc, :].bitcast(F32),
                                        ALU.subtract).then_inc(sem("low_dve"), 1)
                    lows[0] += 1

            def split_low(name, which=(0, 1)):
                n, src, high, low = splits[name]
                for i in which:
                    c = halves(src)[i]
                    dve.wait_ge(sem("x_high"), 2 * n - 1 + i)
                    V.tensor_tensor(low[:, c, :], src[:, c, :], high[:, c, :].bitcast(F32),
                                    ALU.subtract).then_inc(sem("x_split"), 1)

            def bcast(b, n):
                return b.rearrange("p (o t) -> p o t", o=1).to_broadcast([P, n, T])

            def norm_centre(n):
                dve.wait_ge(sem("ln_mean"), n.c)
                V.tensor_tensor(n.src, n.src, bcast(bank[4][:, 0:T], DC), ALU.subtract).then_inc(sem("ln_cen"), 1)
                dve.wait_ge(sem("ln_cen"), n.c)

            def norm_finish(n, affine=True):
                dve.wait_ge(sem("ln_std"), n.n)
                link(V.reciprocal(rstd[:, :], rstd[:, :]))
                mid = n.src if n.c else n.dst
                for i, half_chunks in enumerate(halves(mid)):
                    src, m = n.src[:, half_chunks, :], mid[:, half_chunks, :]
                    ins = V.tensor_tensor(m, src, bcast(rstd[:, :], DC // 2), ALU.mult)
                    if affine:
                        link(ins)
                        for c in range(half_chunks.start, half_chunks.stop):
                            if n.b:
                                ins = V.tensor_scalar(n.dst[:, c, :], mid[:, c, :], n.g(c), n.b(c), ALU.mult, ALU.add)
                            else:
                                ins = V.tensor_scalar(n.dst[:, c, :], mid[:, c, :], n.g(c), None, ALU.mult)
                    ins.then_inc(sem("ln_out"), 1)
                dve.wait_ge(sem("ln_out"), 2 * n.n)

            def ada_tile(i):
                t = ada[i]
                dve.wait_ge(loaded[t.slot], t.loaded)
                if i == 0:
                    dve.wait_ge(sem("pooled_ready"), len(WINDOWS))
                if i >= 2:
                    dve.wait_ge(sem("ada_reduced"), i - 1)
                o = ada_acc[i % 2]
                link(V.tensor_scalar(o, at(t)[:, 0, :], silu_c[:, 0:1], None, ALU.mult))
                for k in range(1, DC):
                    ins = V.scalar_tensor_tensor(out=o, in0=at(t)[:, k, :], scalar=silu_c[:, k:k + 1], in1=o,
                                                 op0=ALU.mult, op1=ALU.add)
                    if k < DC - 1:
                        link(ins)
                ins.then_inc(sem("ada_taken"), 1)
                dve.wait_ge(sem("ada_taken"), i + 1)

            def add_residual(blocks):
                for b, i in blocks:
                    for j, g in enumerate(b.groups):
                        low_until(ahead(g))
                        dve.wait_ge(sem("mm_done"), plan.done[g])
                        c = 4 * i + 2 * j
                        V.scalar_tensor_tensor(out=resid[:, c:c + 2, :], in0=xT[:, c:c + 2, :], scalar=ALPHA,
                                               in1=half(bank[g % BANKS][:, :]), op0=ALU.mult,
                                               op1=ALU.add).then_inc(evac[g % BANKS], 1)

            V.memset(ones[:, :], 1.0).then_inc(sem("consts_set"), 1)
            V.memset(mean_w[:, :], 1.0 / D)
            V.memset(mean_v[:, :], 1.0 / RV).then_inc(sem("consts_set"), 1)
            V.memset(eps[:, 0:1], LN_EPS)
            V.memset(eps[:, 1:2], RMS_EPS)
            V.memset(eps[:, 2:3], GN_EPS).then_inc(sem("consts_set"), 1)
            split_low("x")
            dve.wait_ge(sem("par_in"), 16)
            for i, b in enumerate(glu):
                g = b.groups[1]
                low_until(2 * i + 2)
                wait_evac(dve, b.groups[0])
                dve.wait_ge(sem("mm_done"), plan.done[g])
                for ch in range(2):
                    ins = V.scalar_tensor_tensor(out=a_pad[:, 2 * i + ch, TAPS_A - 1:],
                                                 in0=bank[g % BANKS][:, ch * T:(ch + 1) * T],
                                                 scalar=pc("b_in", 2 * i + ch),
                                                 in1=sg[i % 2][:, ch * T:(ch + 1) * T], op0=ALU.add, op1=ALU.mult)
                ins.then_inc(evac[g % BANKS], 1)
            norm_centre(n_mem)
            dve.wait_ge(sem("pads_zero"), 2)
            wait_evac_all(dve, glu)
            for c in range(DC):
                V.tensor_scalar(conv[:, c, :], a_pad[:, c, 0:T], pc("conv_a_w", c), pc("conv_a_b", c), ALU.mult,
                                ALU.add).then_inc(sem("conv_step"), 1)
            with dve.Fori(1, TAPS_A) as tap:
                for c in range(DC):
                    dve.wait_ge(sem("conv_step"), tap * DC + (c + 1 - DC))
                    V.scalar_tensor_tensor(out=conv[:, c, :], in0=a_pad[:, c, bass.ds(tap, T)],
                                           scalar=par[:, bass.ds(tap * DC + (PCOL["conv_a_w"] + c), 1)],
                                           in1=conv[:, c, :], op0=ALU.mult, op1=ALU.add).then_inc(sem("conv_step"), 1)
            low_until(units_of(branch_gate["c", 0])[1])
            dve.wait_ge(sem("cv_ready"), 4)
            for tap in range(TAPS_B):
                for c in range(DC):
                    if tap == 0:
                        V.tensor_scalar(conv_b[:, c, :], cv_pad[:, c, 0:T], pc("conv_b_w", c), None,
                                        ALU.mult).then_inc(sem("cvb_step"), 1)
                        continue
                    dve.wait_ge(sem("cvb_step"), DC * (tap - 1) + c + 1)
                    V.scalar_tensor_tensor(out=conv_b[:, c, :], in0=cv_pad[:, c, tap:tap + T],
                                           scalar=pc("conv_b_w", tap * DC + c), in1=conv_b[:, c, :], op0=ALU.mult,
                                           op1=ALU.add).then_inc(sem("cvb_step"), 1)
            low_until(units_of(branch_gate["c", 1])[1])
            dve.wait_ge(sem("conv_step"), TAPS_A * DC)
            norm_centre(n_conv)
            dve.wait_ge(sem("silu_c"), 1)
            low_until(units_of(branch_gate["b", 0])[1])
            split_low("gate_b")
            ada_tile(0)
            low_until(units_of(branch_out["b", 0])[1])
            ada_tile(1)
            norm_finish(n_mem)
            low_until(units_of(branch_gate["b", 1])[1])
            norm_finish(n_conv, affine=False)
            ada_tile(2)
            low_until(units_of(branch_out["b", 1])[1])
            ada_tile(3)
            low_until(units_of(branch_gate["a", 0])[1])
            split_low("conv")
            ada_tile(4)
            low_until(units_of(branch_out["a", 0])[1])
            ada_tile(5)
            low_until(units_of(branch_gate["a", 1])[1])
            ada_tile(6)
            low_until(units_of(branch_out["a", 1])[1])
            ada_tile(7)
            low_until(units_of(mix[0])[1])
            split_low("mix")
            split_low("mem")
            ada_tile(8)
            add_residual([(mix[0], 0), (mix[1], 1)])
            ada_tile(9)
            low_until(units_of(xk[0])[1])
            norm_centre(n_1)
            ada_tile(10)
            low_until(units_of(xk[1])[1])
            ada_tile(11)
            norm_finish(n_1)
            split_low("x1")

            def modulation(layer):
                dve.wait_ge(sem("ada_reduced"), 12 * (layer + 1))
                m = slice(48 * layer, 48 * layer + 48)
                link(V.tensor_tensor(mod[:, m], bank[7][:, m], pc("ada_b_2", 48 * layer, 48), ALU.add))
                for k in (2 * layer, 2 * layer + 1):
                    j = 1 + 3 * (k % 2)
                    ins = V.scalar_tensor_tensor(out=gscale[:, DC * k:DC * (k + 1)],
                                                 in0=mod[:, 48 * layer + DC * j:48 * layer + DC * (j + 1)],
                                                 scalar=1.0, in1=pc("norm_gains_2", DC * k, DC), op0=ALU.add,
                                                 op1=ALU.mult)
                ins.then_inc(sem("mod_ready"), 1)

            low_until(units_of(xv[1])[1])
            modulation(0)
            low_until(units_of(xo[0])[1])
            for h in range(XHEADS):
                dve.wait_ge(sem("x_scores"), h + 1)
                link(V.tensor_reduce(xmax[:, 2 * h:2 * h + 2], half(bank[4 + h][:, :]), AX_X, ALU.max))
                V.tensor_scalar(xneg[:, 2 * h:2 * h + 2], xmax[:, 2 * h:2 * h + 2], -XD ** -0.5, None,
                                ALU.mult).then_inc(sem("x_max"), 1)
            for h in range(XHEADS):
                dve.wait_ge(sem("x_exp"), h + 1)
                link(V.reciprocal(xrec[:, 2 * h:2 * h + 2], xsum[:, 2 * h:2 * h + 2]))
                for i in range(TT):
                    ins = V.tensor_scalar(half(prob[h])[:, i, :], half(prob[h])[:, i, :],
                                          xrec[:, 2 * h + i:2 * h + i + 1], None, ALU.mult)
                ins.then_inc(sem("x_prob"), 1)
            split_low("attn")
            add_residual([(xo[0], 0), (xo[1], 1)])
            norm_centre(n_2)
            norm_finish(n_2)

            dve.wait_ge(sem("r_logits"), 1)
            dve.wait_ge(sem("c1_in"), 16)
            link(V.tensor_tensor(lg, bank[5][:, 0:2 * NEXP].rearrange("p (i e) -> p i e", i=2),
                                 k1("router_b", NEXP).rearrange("p (o e) -> p o e", o=1).to_broadcast([P, 2, NEXP]),
                                 ALU.add))
            for i in range(TT):
                ins = V.max(top8[:, i, :], lg[:, i, :])
            link(ins)
            for i in range(TT):
                V.max_index(idx[:, i, :], top8[:, i, :], lg[:, i, :])
            link(V.tensor_scalar(negm[:, 0:2], top8[:, :, 0:1].rearrange("p i e -> p (i e)"), -1.0, None, ALU.mult))
            link(V.tensor_copy(idxf, idx[:, :, :]))
            for k in range(TOPK):
                for i in range(TT):
                    if k == 0:
                        ins = V.tensor_scalar(mask[:, i, :], k1("slot", NEXP), idxf[:, i, 0:1], None, ALU.is_equal)
                    else:
                        ins = V.scalar_tensor_tensor(out=mask[:, i, :], in0=k1("slot", NEXP),
                                                     scalar=idxf[:, i, k:k + 1], in1=mask[:, i, :],
                                                     op0=ALU.is_equal, op1=ALU.add)
                if k < TOPK - 1:
                    link(ins)
            ins.then_inc(sem("r_mask"), 1)
            dve.wait_ge(sem("r_mask"), 1)
            dve.sem_inc(sem("r_top"), 1)
            dve.wait_ge(sem("r_exp"), 1)
            link(V.tensor_tensor(ex, ex, mask, ALU.mult))
            link(V.tensor_reduce(den[:, 0:2], ex, AX_X, ALU.add))
            link(V.reciprocal(rden[:, 0:2], den[:, 0:2]))
            for i in range(TT):
                ins = V.tensor_scalar(gates[:, i, :], ex[:, i, :], rden[:, i:i + 1], None, ALU.mult)
            ins.then_inc(sem("r_gates"), 1)
            dve.wait_ge(sem("r_gates"), 1)
            dve.wait_ge(sem("r_pos"), 1)
            link(V.tensor_reduce(cmax[:, 0:1], bank[6][:, 2 * NEXP:3 * NEXP], AX_X, ALU.max))
            link(V.tensor_scalar(over[:, 0:1], cmax[:, 0:1], float(CAP), 1.0, ALU.is_gt, ALU.add))
            for k in range(2, T // CAP):
                link(V.tensor_scalar(over[:, 1:2], cmax[:, 0:1], float(k * CAP), None, ALU.is_gt))
                link(V.tensor_tensor(over[:, 0:1], over[:, 0:1], over[:, 1:2], ALU.add))
            link(V.tensor_scalar(over[:, 1:2], over[:, 0:1], float(NEXP), -1.0, ALU.mult, ALU.add))
            V.tensor_copy(nrounds[:, :], over[:, 0:2]).then_inc(sem("rounds_ready"), 1)
            link(V.scalar_tensor_tensor(out=posr, in0=bank[6][:, 0:2 * NEXP].rearrange("p (i e) -> p i e", i=2),
                                        scalar=-FAR, in1=mask, op0=ALU.add, op1=ALU.mult))
            link(V.tensor_scalar(posr, posr, FAR, None, ALU.add))
            for q in range(4):
                dve.wait_ge(sem("r_bias"), q + 1)
                V.scalar_tensor_tensor(out=acc[:, 2 * q:2 * q + 2, :], in0=xT[:, 2 * q:2 * q + 2, :], scalar=ALPHA,
                                       in1=half(bank[q][:, :]), op0=ALU.mult, op1=ALU.add).then_inc(sem("m_acc"), 1)
            dve.wait_ge(sem("m_acc"), 4)
            dve.wait_ge(sem("rounds_ready"), 1)
            n = dve.value_load(nrounds[0:1, 0:1], min_val=1, max_val=T // CAP)
            slot = k1("slot")

            def select(e):
                for i in range(TT):
                    ins = V.tensor_scalar(Ssel[i], slot[:, 0:CAP], posr[:, i, bass.ds(e, 1)], None, ALU.is_equal)
                ins.then_inc(sem("m_sel"), 1)

            def select_gated(it, e):
                for i in range(TT):
                    ins = V.tensor_scalar(Gsel[i], slot, posr[:, i, bass.ds(e, 1)], gates[:, i, bass.ds(e, 1)],
                                          ALU.is_equal, ALU.mult)
                ins.then_inc(sem("m_gsel"), 1)

            def activate(it, e, b):
                tv = gu_t[b].rearrange("p (c j) -> p c j", c=8)
                gate = gu_t[b].rearrange("p (c g j) -> p c g j", c=4, g=2)[:, :, 0, :]
                up = gu_t[b].rearrange("p (c g j) -> p c g j", c=4, g=2)[:, :, 1, :]
                bias = par[:, bass.ds(e * 16 + (PCOL["b_gu"] + 8 * b), 8)].rearrange(
                    "p (c o) -> p c o", o=1).to_broadcast([P, 8, CAP])
                dve.wait_ge(sem("m_guturn"), it * 2 + (b + 1))
                V.tensor_tensor(tv, bank[2 + b][:, :].rearrange("p (c j) -> p c j", c=8), bias,
                                ALU.add).then_inc(sem("m_vec"), 1)
                dve.wait_ge(sem("m_vec"), it * 6 + (3 * b + 1))
                V.tensor_scalar(gate, gate, LIMIT, None, ALU.min).then_inc(sem("m_gate"), 1)
                V.tensor_scalar(up, up, LIMIT, -LIMIT, ALU.min, ALU.max).then_inc(sem("m_vec"), 1)
                dve.wait_ge(sem("m_vec"), it * 6 + (3 * b + 2))
                dve.wait_ge(sem("m_gate"), it * 2 + (b + 1))
                V.scalar_tensor_tensor(out=up, in0=up, scalar=1.0, in1=gate, op0=ALU.add,
                                       op1=ALU.mult).then_inc(sem("m_vec"), 1)
                dve.wait_ge(sem("m_vec"), it * 6 + (3 * b + 3))
                dve.wait_ge(sem("m_sig"), it * 2 + (b + 1))
                V.tensor_tensor(actT[:, 4 * b:4 * b + 4, :], up, sig[b].rearrange("p (c j) -> p c j", c=4),
                                ALU.mult).then_inc(sem("m_act"), 1)

            def accumulate(it):
                for q in range(4):
                    dve.wait_ge(sem("m_scatter"), it * 4 + (q + 1))
                    V.tensor_tensor(acc[:, 2 * q:2 * q + 2, :], acc[:, 2 * q:2 * q + 2, :],
                                    half(bank[4 + q][:, :]), ALU.add).then_inc(sem("m_acc"), 1)
                dve.wait_ge(sem("m_acc"), it * 4 + 8)

            select(0)
            with dve.Fori(0, n) as r:
                with dve.Fori(0, NEXP - 1) as e:
                    it = r * NEXP + e
                    select_gated(it, e)
                    dve.wait_ge(sem("m_gather"), it + 1)
                    select(e + 1)
                    activate(it, e, 0)
                    activate(it, e, 1)
                    accumulate(it)
                it = r * NEXP + (NEXP - 1)
                select_gated(it, NEXP - 1)
                dve.wait_ge(sem("m_gather"), it + 1)
                dve.wait_ge(sem("m_gsel"), it + 1)
                V.tensor_scalar(posr, posr, -float(CAP), None, ALU.add).then_inc(sem("m_round"), 1)
                dve.wait_ge(sem("m_round"), r + 1)
                select(0)
                activate(it, NEXP - 1, 0)
                activate(it, NEXP - 1, 1)
                accumulate(it)
            norm_centre(n_3)
            norm_finish(n_3)

            dve.wait_ge(sem("mod_ready"), 1)
            low_until(units_of(aq[0])[1])
            norm_finish(rms[0])
            split_low("h0")
            low_until(units_of(ao[0])[1])
            dve.wait_ge(sem("c2_in"), 32)
            for n_, (X, blocks) in enumerate(((q2, aq), (kk2, ak))):
                wait_evac_all(dve, blocks)
                for p_ in range(2):
                    c = 4 + 2 * p_
                    dve.wait_ge(sem("rope_mm"), 2 * n_ + p_ + 1)
                    link(V.tensor_tensor(half(rope_t), half(bank[4 + 2 * n_ + p_][:, :]), bcast(k2("rope_sin", T), 2),
                                         ALU.mult))
                    link(V.tensor_tensor(X[:, c:c + 2, :], X[:, c:c + 2, :], bcast(k2("rope_cos", T), 2), ALU.mult))
                    V.tensor_tensor(X[:, c:c + 2, :], X[:, c:c + 2, :], half(rope_t), ALU.add).then_inc(sem("roped"), 1)
                    dve.wait_ge(sem("roped"), 2 * n_ + p_ + 1)

            def diag(b):
                return b.rearrange("p (k j) -> p k j", k=3)[:, 0:3:2, :]

            def mask2(name):
                return k2(name).rearrange("p (o j) -> p o j", o=1).to_broadcast([P, 2, P])

            for i in range(NSB + 2):
                if i < NSB:
                    k = i % 2
                    dve.wait_ge(sem("a_sp"), i + 1)
                    if i >= 2:
                        dve.wait_ge(sem("a_after"), i - 1)
                        dve.wait_ge(sem("a_exp"), i - 1)
                    link(V.tensor_tensor(a_L[k], a_r[k], a_e[k], ALU.add))
                    link(V.scalar_tensor_tensor(out=a_t[k], in0=bank[4 + k][:, 0:384], scalar=HD ** -0.5, in1=a_L[k],
                                                op0=ALU.mult, op1=ALU.subtract))
                    V.tensor_tensor(diag(a_L[k]), diag(a_L[k]), mask2("strict"), ALU.mult).then_inc(sem("a_L"), 1)
                if 1 <= i <= NSB:
                    h = i - 1
                    k = h % 2
                    dve.wait_ge(sem("a_after"), h + 1)
                    V.tensor_tensor(a_t[k], a_t[k], bank[6][:, 0:384], ALU.subtract).then_inc(sem("a_t"), 1)
                    dve.wait_ge(sem("a_exp"), h + 1)
                    V.tensor_tensor(diag(a_A[k]), diag(a_A[k]), mask2("strict"), ALU.mult).then_inc(sem("a_A"), 1)
                if i >= 3 and i % 2:
                    h = i - 2
                    dve.wait_ge(sem("a_o"), h + 1)
                    V.tensor_copy(attn2[:, h // 2, :], bank[7][:, 0:T]).then_inc(sem("a_oT"), 1)
            dve.wait_ge(sem("a_A"), NSB)
            for i in range(NSB + 2):
                if i < NSB:
                    k = i % 2
                    dve.wait_ge(sem("b_s"), i + 1)
                    if i >= 2:
                        dve.wait_ge(sem("b_exp"), i - 1)
                    link(V.tensor_scalar(a_L[k], bank[4 + k][:, 0:384], HD ** -0.5, None, ALU.mult))
                    link(V.tensor_tensor(diag(a_L[k]), diag(a_L[k]), mask2("causal"), ALU.add))
                    V.tensor_reduce(bmax[:, 2 * k:2 * k + 1], a_L[k][:, 0:P], AX_X, ALU.max)
                    link(V.tensor_reduce(bmax[:, 2 * k + 1:2 * k + 2], a_L[k][:, P:P + T], AX_X, ALU.max))
                    V.tensor_scalar(bneg[:, 2 * k:2 * k + 2], bmax[:, 2 * k:2 * k + 2], -1.0, None,
                                    ALU.mult).then_inc(sem("b_max"), 1)
                if 1 <= i <= NSB:
                    h = i - 1
                    k = h % 2
                    dve.wait_ge(sem("b_exp"), h + 1)
                    link(V.reciprocal(brec[:, 2 * k:2 * k + 2], bsum[:, 2 * k:2 * k + 2]))
                    V.tensor_scalar(a_t[k][:, 0:P], a_t[k][:, 0:P], brec[:, 2 * k:2 * k + 1], None, ALU.mult)
                    V.tensor_scalar(a_t[k][:, P:P + T], a_t[k][:, P:P + T], brec[:, 2 * k + 1:2 * k + 2], None,
                                    ALU.mult).then_inc(sem("b_prob"), 1)
                if i >= 3 and i % 2:
                    h = i - 2
                    dve.wait_ge(sem("b_o"), h + 1)
                    V.tensor_copy(attn2[:, NSB // 2 + h // 2, :], bank[7][:, 0:T]).then_inc(sem("b_oT"), 1)

            def add_gated(blocks, gate, first=0):
                for i, b in enumerate(blocks, first):
                    for j, g in enumerate(b.groups):
                        low_until(ahead(g))
                        dve.wait_ge(sem("mm_done"), plan.done[g])
                        for ch in range(2):
                            c = 4 * i + 2 * j + ch
                            ins = V.scalar_tensor_tensor(out=xT[:, c, :], in0=bank[g % BANKS][:, ch * T:(ch + 1) * T],
                                                         scalar=gate(c), in1=xT[:, c, :], op0=ALU.mult, op1=ALU.add)
                        ins.then_inc(evac[g % BANKS], 1)
                wait_evac_all(dve, blocks)

            def feed_forward(layer):
                low_until(units_of(gate_up[layer][0])[1])
                norm_finish(rms[2 * layer + 1])
                split_low(("h1", "h3")[layer])
                for i, b in enumerate(gate_up[layer]):
                    g = b.groups[1]
                    low_until(ahead(g))
                    wait_evac(dve, b.groups[0])
                    dve.wait_ge(sem("mm_done"), plan.done[g])
                    V.tensor_tensor(ff_h[i % 2], bank[g % BANKS][:, :], ff_s[i % 2],
                                    ALU.mult).then_inc(evac[g % BANKS], 1)
                    wait_evac(dve, g)
                    high, low = (hidden[k][:, 2 * i:2 * i + 2, :] for k in range(2))
                    link(V.tensor_copy(high, half(ff_h[i % 2])))
                    V.tensor_tensor(low, half(ff_h[i % 2]), high.bitcast(F32),
                                    ALU.subtract).then_inc(sem("ff_hidden"), 1)
                    if layer == 0:
                        ada_tile(12 + i)
                if layer == 0:
                    add_gated(down[0][:1], mcol(0, 5))
                    ada_tile(23)
                    add_gated(down[0][1:], mcol(0, 5), 1)
                    modulation(1)
                else:
                    add_gated(down[layer], mcol(layer, 5))

            split_low("attn2")
            add_gated(ao, mcol(0, 2))
            feed_forward(0)
            low_until(units_of(rq[0])[1])
            norm_finish(rms[2])
            split_low("h2")
            for n_, (X, blocks) in enumerate(((q2, rq), (kk2, rk))):
                low_until(units_of(blocks[-1])[1] + 2)
                wait_evac_all(dve, blocks)
                hv = X.rearrange("p (h s) t -> p h s t", s=2)
                x1, x2 = hv[:, :, 0, :], hv[:, :, 1, :]
                cos, sin = bcast(k2("ret_cos", T), RH), bcast(k2("ret_sin", T), RH)
                link(V.tensor_tensor(rot_t[0], x2, sin, ALU.mult))
                link(V.tensor_tensor(rot_t[1], x1, sin, ALU.mult))
                link(V.tensor_tensor(x1, x1, cos, ALU.mult))
                link(V.tensor_tensor(x2, x2, cos, ALU.mult))
                link(V.tensor_tensor(x1, x1, rot_t[0], ALU.subtract))
                V.tensor_tensor(x2, x2, rot_t[1], ALU.add).then_inc(sem("ret_rot"), 1)
                dve.wait_ge(sem("ret_rot"), n_ + 1)
            low_until(units_of(ro[0])[1])
            for h in range(RH):
                k = h % 2
                dve.wait_ge(sem("ret_s"), h + 1)
                if h >= 2:
                    dve.wait_ge(sem("ret_omm"), 2 * (h - 1))
                V.tensor_tensor(att_a[k][:, 0:T], bank[4 + k][:, 0:T], dec[:, h, :], ALU.mult)
                V.tensor_tensor(att_a[k][:, T:T + P], bank[4 + k][:, T:T + P], dec[:, h, 0:P],
                                ALU.mult).then_inc(sem("ret_inner"), 1)
            for h in range(RH):
                dve.wait_ge(sem("gn_mean"), h // 2 + 1)
                oh = ret_o[:, 4 * h:4 * h + 4, :]
                V.tensor_tensor(oh, oh, bcast(bank[4 + h // 2][:, (h % 2) * T:(h % 2 + 1) * T], 4),
                                ALU.subtract).then_inc(sem("gn_cen"), 1)
            dve.wait_ge(sem("gn_cen"), RH)
            for hp in range(2):
                dve.wait_ge(sem("gn_std"), hp + 1)
                pair = gn_std[:, 2 * hp:2 * hp + 2, :]
                link(V.reciprocal(pair, pair))
                for h in (2 * hp, 2 * hp + 1):
                    oh = ret_o[:, 4 * h:4 * h + 4, :]
                    ins = V.tensor_tensor(oh, oh, bcast(gn_std[:, h, :], 4), ALU.mult)
                link(ins)
                if hp:
                    split_low("ret", (0,))
                for c in range(8 * hp, 8 * hp + 8):
                    ins = V.scalar_tensor_tensor(out=ret_o[:, c, :], in0=ret_o[:, c, :], scalar=pc("ret_gn_2", c),
                                                 in1=ret_g[:, c, :], op0=ALU.mult, op1=ALU.mult)
                ins.then_inc(sem("gn_out"), 1)
            dve.wait_ge(sem("gn_out"), 2)
            split_low("ret", (1,))
            add_gated(ro, mcol(1, 2))
            feed_forward(1)
            norm_finish(n_end)

        @block.gpsimd
        def _(pool):
            steps = [0]

            def link(ins):
                steps[0] += 1
                ins.then_inc(sem("pool_step"), 1)
                pool.wait_ge(sem("pool_step"), steps[0])

            G = nc.gpsimd
            lows = [0]

            def low_until(n):
                while lows[0] <= n:
                    u = plan.units[lows[0]]
                    if u.low == "low_pool":
                        pool.wait_ge(sem("w_high"), u.n + 1)
                        G.tensor_tensor(low_part(u)[:, 0:u.kc, :], at(u.tile)[:, 0:u.kc, u.j * HALF:(u.j + 1) * HALF],
                                        w_high[u.n % HIGHS][:, 0:u.kc, :].bitcast(F32),
                                        ALU.subtract).then_inc(sem("low_pool"), 1)
                    lows[0] += 1

            G.memset(a_pad[:, :, 0:TAPS_A - 1], 0.0).then_inc(sem("pads_zero"), 1)
            G.memset(cv_pad[:, :, 0:TAPS_B - 1], 0.0).then_inc(sem("pads_zero"), 1)
            for i, b in enumerate(cv):
                low_until(b.units[1].n + 1)
                wait_evac(pool, b.groups[0])
                wait_evac(pool, b.groups[1])
                G.tensor_tensor(cv_pad[:, 2 * i:2 * i + 2, TAPS_B - 1:], half(sg[i % 2]), half(yb[i % 2]),
                                ALU.mult).then_inc(sem("cv_ready"), 1)
            pool.wait_ge(sem("cv_ready"), 4)
            link(G.memset(pool_in[:, :, 0:PADW], 0.0))
            pool.wait_ge(sem("c1_in"), 16)
            low_until(units_of(gb[0])[1])
            wait_evac_all(pool, pi)
            for k, w in enumerate(WINDOWS):
                if k >= 2:
                    low_until(units_of(gb[1])[k - 2])
                u = pool_in[:, 2 * k:2 * k + 2, :]
                src, shift = u, 1
                while shift < w:
                    dst = win[(shift.bit_length() - 1) % 2]
                    first = 2 * shift - 1
                    link(G.tensor_tensor(dst[:, :, first:], src[:, :, first:], src[:, :, first - shift:T + PADW - shift],
                                         ALU.add))
                    src, shift = dst, 2 * shift
                count = c1[:, C1["count"] + k * T:C1["count"] + (k + 1) * T].rearrange(
                    "p (o t) -> p o t", o=1).to_broadcast([P, 2, T])
                link(G.tensor_tensor(pooled[:, 2 * k:2 * k + 2, :], src[:, :, PADW:], count, ALU.mult))
                G.tensor_tensor(pooled[:, 2 * k:2 * k + 2, :], pooled[:, 2 * k:2 * k + 2, :], u[:, :, PADW:],
                                ALU.subtract).then_inc(sem("pooled_ready"), 1)
                pool.wait_ge(sem("pooled_ready"), k + 1)

            def mix_in(name, k, i):
                for j in range(2):
                    n = 4 * k + 2 * i + j
                    wait_evac(pool, branch_gate[name, i].groups[j])
                    wait_evac(pool, branch_out[name, i].groups[j])
                    m = m_sum[:, 4 * i + 2 * j:4 * i + 2 * j + 2, :]
                    if k == 0:
                        G.tensor_tensor(m, half(sg[n % 2]), half(yb[n % 2]), ALU.mult).then_inc(sem("mixed"), 1)
                    else:
                        link(G.tensor_tensor(yb[n % 2], sg[n % 2], yb[n % 2], ALU.mult))
                        G.tensor_tensor(m, m, half(yb[n % 2]), ALU.add).then_inc(sem("mixed"), 1)
                    pool.wait_ge(sem("mixed"), n + 1)

            wait_evac_all(pool, gb)
            mix_in("c", 0, 0)
            mix_in("c", 0, 1)
            pool.wait_ge(sem("cvb_step"), TAPS_B * DC)
            G.tensor_tensor(gate_b, gate_b, conv_b, ALU.mult).then_inc(sem("gated"), 1)
            low_until(units_of(branch_gate["b", 1])[0])
            mix_in("b", 1, 0)
            low_until(units_of(branch_gate["a", 0])[0])
            mix_in("b", 1, 1)
            low_until(units_of(branch_gate["a", 1])[0])
            mix_in("a", 2, 0)
            low_until(units_of(mix[0])[0])
            mix_in("a", 2, 1)
            low_until(len(plan.units) - 1)


def _columns(v):
    return np.ascontiguousarray(np.asarray(v).reshape(-1, P).T)


def _constants():
    i = np.arange(P)
    t = np.arange(T)
    one = {
        "ident": np.eye(P),
        "later": (i[:, None] > i[None, :]),
        "before": (i[:, None] < i[None, :]),
        "slot": np.tile(np.arange(CAP), (P, 2)),
        "count": np.tile(np.concatenate([1.0 / np.minimum(t + 1, w) for w in WINDOWS]), (P, 1)),
    }

    def angles(d, rows):
        inv = np.float32(10000.0) ** (-np.arange(0, d, 2, dtype=np.float32) / np.float32(d))
        return (t.astype(np.float32)[None, :] * inv[rows][:, None]).astype(np.float32)

    ret, rope = angles(XD, i), angles(HD, i % (HD // 2))
    swap = np.zeros((P, P))
    for m in range(P):
        if m % HD < HD // 2:
            swap[m + HD // 2, m] = -1.0
        else:
            swap[m - HD // 2, m] = 1.0
    two = {
        "ret_cos": np.cos(ret), "ret_sin": np.sin(ret), "rope_cos": np.cos(rope), "rope_sin": np.sin(rope),
        "swap": swap, "strict": (i[:, None] < i[None, :]), "causal": np.where(i[None, :] <= i[:, None], 0.0, NEG),
    }
    diff = t[None, :] - i[:, None]
    gamma = np.log(1.0 - 2.0 ** (-5.0 - np.arange(RH)))
    decay = [np.where(diff >= 0, np.exp(g * np.maximum(diff, 0)), 0.0) * XD ** -0.5 for g in gamma]
    return one, two, np.concatenate(decay, axis=1).astype(np.float32)


WEIGHTS = ["w_in", "w_a_out", "w_b_out", "pool_w", "w_mix_out", "w_xq", "w_xk", "w_xv", "w_xo", "router_w", "w_gu",
           "w_down", "b_down", "ada_w_2", "att_w_qkv_2", "att_w_o_2", "ret_w_in_2", "ret_w_o_2",
           "ffn_w_gate_up_2", "ffn_w_down_2"]


def kernel(**inputs):
    from concourse import bacc
    from concourse.bass_utils import run_bass_kernel_spmd

    arrays = {name: np.ascontiguousarray(inputs[name]) for name in WEIGHTS}
    arrays["xT"] = np.ascontiguousarray(np.asarray(inputs["x"])[0].T)
    arrays["memT"] = np.ascontiguousarray(np.asarray(inputs["mem"])[0].T)
    cols = {name: _columns(inputs[name]) for name, _ in PARAMS if name != "b_gu"}
    cols["b_gu"] = np.asarray(inputs["b_gu"])[0].reshape(NEXP, 2, 2, 4, P).transpose(4, 0, 2, 3, 1).reshape(P, -1)
    arrays["params"] = np.ascontiguousarray(np.concatenate([cols[name] for name, _ in PARAMS], axis=1))
    one, two, decay = _constants()
    one["router_b"] = np.repeat(np.asarray(inputs["router_b"]), P, axis=0)
    arrays["consts1"] = np.concatenate([one[name] for name, _ in CONST1], axis=1).astype(np.float32)
    arrays["consts2"] = np.concatenate([two[name] for name, _ in CONST2], axis=1).astype(np.float32)
    arrays["decay"] = decay

    nc = bacc.Bacc("TRN2", target_bir_lowering=False, num_devices=1)
    aps = {name: nc.dram_tensor(name, v.shape, mybir.dt.from_np(v.dtype), kind="ExternalInput").ap()
           for name, v in arrays.items()}
    out = nc.dram_tensor("outT", (D, T), F32, kind="ExternalOutput").ap()
    build_program(nc, aps, aps["consts1"], aps["consts2"], aps["decay"], aps["params"], out)
    r = run_bass_kernel_spmd(nc, [arrays], core_ids=[0])
    return np.ascontiguousarray(r.results[0]["outT"].T)[None]
```
